# Optimizing a Trainium2 kernel written in Bass

```python
import jax, jax.numpy as jnp
from jax import lax
import numpy as np

D_MODEL = 1024
BATCH = 1
SEQ = 256
DEPTH = 2

HEAD_DIM = 64
ROPE_THETA = 10000.0
NORM_EPS = 1e-6
A_HEADS = 8
IDX_HEADS = 4
IDX_DIM = 64
IDX_TOPK_MAX = 256
B_HEADS = 8
B_KV_HEADS = 2
WINDOW = 128
C_HEADS = 8
MOBA_BLOCK = 256
MOBA_TOPK = 3
C_Q_CHUNK = 64
Q_BLOCK = 128
N_BRANCH = 3
BRANCH_WIDTH = 8 * HEAD_DIM
D_FF = 4 * D_MODEL
IN_SIZES = (
    A_HEADS * HEAD_DIM, HEAD_DIM, HEAD_DIM,
    IDX_HEADS * IDX_DIM, IDX_DIM, IDX_HEADS,
    B_HEADS * HEAD_DIM, B_KV_HEADS * HEAD_DIM, B_KV_HEADS * HEAD_DIM,
    C_HEADS * HEAD_DIM, C_HEADS * HEAD_DIM, C_HEADS * HEAD_DIM,
    N_BRANCH * D_MODEL,
)
N_IN = sum(IN_SIZES)

kernel_name = 'hybrid_dsa_swa_moba_gated_block'

def rms_norm(x, g):
    xf = x.astype(jnp.float32)
    y = xf * lax.rsqrt(jnp.mean(xf * xf, axis=-1, keepdims=True) + NORM_EPS)
    return (y * g.astype(jnp.float32)).astype(x.dtype)

def rope_tables(seq, dim):
    inv = 1.0 / (ROPE_THETA ** (jnp.arange(0, dim, 2, dtype=jnp.float32) / dim))
    ang = jnp.arange(seq, dtype=jnp.float32)[:, None] * inv[None, :]
    return jnp.cos(ang), jnp.sin(ang)

def apply_rope(x, cos, sin):
    half = x.shape[-1] // 2
    x1, x2 = x[..., :half], x[..., half:]
    c = cos[None, :, None, :].astype(x.dtype)
    s = sin[None, :, None, :].astype(x.dtype)
    return jnp.concatenate([x1 * c - x2 * s, x1 * s + x2 * c], axis=-1)

def dsa_attention(q, k, v, q_idx, k_idx, w_idx):
    b, s, h, d = q.shape
    top_k = min(IDX_TOPK_MAX, s // 4)
    key_pos = jnp.arange(s)
    idx_scale = (IDX_DIM ** -0.5) * (IDX_HEADS ** -0.5)
    att_scale = d ** -0.5

    def one_block(i):
        start = i * Q_BLOCK
        qb = lax.dynamic_slice_in_dim(q, start, Q_BLOCK, axis=1)
        qib = lax.dynamic_slice_in_dim(q_idx, start, Q_BLOCK, axis=1)
        wb = lax.dynamic_slice_in_dim(w_idx, start, Q_BLOCK, axis=1)
        qpos = start + jnp.arange(Q_BLOCK)
        dots = jnp.einsum('bqhe,bse->bqhs', qib, k_idx).astype(jnp.float32)
        score = jnp.einsum('bqh,bqhs->bqs', wb.astype(jnp.float32), jax.nn.relu(dots)) * idx_scale
        causal = key_pos[None, :] <= qpos[:, None]
        score = jnp.where(causal[None], score, -jnp.inf)
        _, sel = lax.top_k(score, top_k)
        valid = sel <= qpos[None, :, None]
        k_sel = jax.vmap(lambda kk, ii: kk[ii])(k, sel)
        v_sel = jax.vmap(lambda vv, ii: vv[ii])(v, sel)
        logits = jnp.einsum('bqhd,bqkd->bqhk', qb, k_sel).astype(jnp.float32) * att_scale
        logits = jnp.where(valid[:, :, None, :], logits, -jnp.inf)
        p = jax.nn.softmax(logits, axis=-1).astype(v.dtype)
        return jnp.einsum('bqhk,bqkd->bqhd', p, v_sel)

    out = lax.map(one_block, jnp.arange(s // Q_BLOCK))
    return out.transpose(1, 0, 2, 3, 4).reshape(b, s, h * d)

def swa_sink_attention(q, k, v, sinks):
    b, s, hq, d = q.shape
    hkv = k.shape[2]
    g = hq // hkv
    nq = s // WINDOW
    qb = q.reshape(b, nq, WINDOW, hkv, g, d)
    pad = ((0, 0), (WINDOW, 0), (0, 0), (0, 0))
    kp = jnp.pad(k, pad).reshape(b, nq + 1, WINDOW, hkv, d)
    vp = jnp.pad(v, pad).reshape(b, nq + 1, WINDOW, hkv, d)
    kb = jnp.concatenate([kp[:, :-1], kp[:, 1:]], axis=2)
    vb = jnp.concatenate([vp[:, :-1], vp[:, 1:]], axis=2)
    logits = jnp.einsum('bnqhgd,bnkhd->bnhgqk', qb, kb).astype(jnp.float32) * (d ** -0.5)
    qpos = jnp.arange(nq)[:, None] * WINDOW + jnp.arange(WINDOW)[None, :]
    kpos = jnp.arange(nq)[:, None] * WINDOW - WINDOW + jnp.arange(2 * WINDOW)[None, :]
    diff = qpos[:, :, None] - kpos[:, None, :]
    mask = (diff >= 0) & (diff < WINDOW) & (kpos[:, None, :] >= 0)
    logits = jnp.where(mask[None, :, None, None], logits, -jnp.inf)
    sink = sinks.astype(jnp.float32).reshape(hkv, g)[None, None, :, :, None, None]
    sink = jnp.broadcast_to(sink, logits.shape[:-1] + (1,))
    p = jax.nn.softmax(jnp.concatenate([logits, sink], axis=-1), axis=-1)[..., :-1]
    out = jnp.einsum('bnhgqk,bnkhd->bnqhgd', p.astype(v.dtype), vb)
    return out.reshape(b, s, hq * d)

def moba_attention(q, k, v):
    b, s, h, d = q.shape
    nkb = -(-s // MOBA_BLOCK)
    pad = nkb * MOBA_BLOCK - s
    padw = ((0, 0), (0, pad), (0, 0), (0, 0))
    kbl = jnp.pad(k, padw).reshape(b, nkb, MOBA_BLOCK, h, d).transpose(0, 3, 1, 2, 4)
    vbl = jnp.pad(v, padw).reshape(b, nkb, MOBA_BLOCK, h, d).transpose(0, 3, 1, 2, 4)
    kmean = jnp.mean(kbl.astype(jnp.float32), axis=3)
    n_sel = min(MOBA_TOPK, nkb - 1)
    scale = d ** -0.5
    bi = jnp.arange(b)[:, None, None, None]
    hi = jnp.arange(h)[None, :, None, None]
    blk_ids = jnp.arange(nkb)

    def one_chunk(c):
        start = c * C_Q_CHUNK
        qc = lax.dynamic_slice_in_dim(q, start, C_Q_CHUNK, axis=1).transpose(0, 2, 1, 3)
        qpos = start + jnp.arange(C_Q_CHUNK)
        own = start // MOBA_BLOCK
        k_own = lax.dynamic_index_in_dim(kbl, own, axis=2, keepdims=False)
        v_own = lax.dynamic_index_in_dim(vbl, own, axis=2, keepdims=False)
        kpos_own = own * MOBA_BLOCK + jnp.arange(MOBA_BLOCK)
        l_own = jnp.einsum('bhqd,bhkd->bhqk', qc, k_own).astype(jnp.float32) * scale
        l_own = jnp.where((kpos_own[None, :] <= qpos[:, None])[None, None], l_own, -jnp.inf)
        if n_sel == 0:
            p_own = jax.nn.softmax(l_own, axis=-1).astype(v.dtype)
            out = jnp.einsum('bhqk,bhkd->bhqd', p_own, v_own)
            return out.transpose(0, 2, 1, 3)
        gate = jnp.einsum('bhqd,bhnd->bhqn', qc.astype(jnp.float32), kmean)
        gate = jnp.where((blk_ids < own)[None, None, None, :], gate, -jnp.inf)
        _, sel = lax.top_k(gate, n_sel)
        valid = sel < own
        k_sel = kbl[bi, hi, sel]
        v_sel = vbl[bi, hi, sel]
        l_sel = jnp.einsum('bhqd,bhqnkd->bhqnk', qc, k_sel).astype(jnp.float32) * scale
        l_sel = jnp.where(valid[..., None], l_sel, -jnp.inf).reshape(b, h, C_Q_CHUNK, n_sel * MOBA_BLOCK)
        p = jax.nn.softmax(jnp.concatenate([l_sel, l_own], axis=-1), axis=-1).astype(v.dtype)
        p_sel = p[..., :n_sel * MOBA_BLOCK].reshape(b, h, C_Q_CHUNK, n_sel, MOBA_BLOCK)
        p_own = p[..., n_sel * MOBA_BLOCK:]
        out = (jnp.einsum('bhqnk,bhqnkd->bhqd', p_sel, v_sel)
               + jnp.einsum('bhqk,bhkd->bhqd', p_own, v_own))
        return out.transpose(0, 2, 1, 3)

    out = lax.map(one_chunk, jnp.arange(s // C_Q_CHUNK))
    return out.transpose(1, 0, 2, 3, 4).reshape(b, s, h * d)

def hybrid_layer(x, cos, sin, norm1, w_in, sinks, w_branch, w_out, norm2, w_ff1, w_ff2):
    b, s, _ = x.shape
    h = rms_norm(x, norm1)
    proj = h @ w_in
    split_points = np.cumsum(np.array(IN_SIZES))[:-1].tolist()
    (aq, ak, av, iq, ik, iw, bq, bk, bv, cq, ck, cv, gates) = jnp.split(proj, split_points, axis=-1)

    aq = apply_rope(aq.reshape(b, s, A_HEADS, HEAD_DIM), cos, sin)
    ak = apply_rope(ak[:, :, None, :], cos, sin)[:, :, 0, :]
    iq = apply_rope(iq.reshape(b, s, IDX_HEADS, IDX_DIM), cos, sin)
    ik = apply_rope(ik[:, :, None, :], cos, sin)[:, :, 0, :]
    o_a = dsa_attention(aq, ak, av, iq, ik, iw)

    bq = apply_rope(bq.reshape(b, s, B_HEADS, HEAD_DIM), cos, sin)
    bk = apply_rope(bk.reshape(b, s, B_KV_HEADS, HEAD_DIM), cos, sin)
    bv = bv.reshape(b, s, B_KV_HEADS, HEAD_DIM)
    o_b = swa_sink_attention(bq, bk, bv, sinks)

    cq = apply_rope(cq.reshape(b, s, C_HEADS, HEAD_DIM), cos, sin)
    ck = apply_rope(ck.reshape(b, s, C_HEADS, HEAD_DIM), cos, sin)
    cv = cv.reshape(b, s, C_HEADS, HEAD_DIM)
    o_c = moba_attention(cq, ck, cv)

    branches = jnp.stack([o_a, o_b, o_c], axis=2)
    g = jax.nn.sigmoid(gates.reshape(b, s, N_BRANCH, D_MODEL))
    merged = jnp.sum(g * jnp.einsum('bsnc,ncd->bsnd', branches, w_branch), axis=2)
    x = x + merged @ w_out

    h2 = rms_norm(x, norm2)
    x = x + jnp.square(jax.nn.relu(h2 @ w_ff1)) @ w_ff2
    return x

def setup_inputs(seed: int = 0) -> dict:
    key = jax.random.key(seed)
    ks = jax.random.split(key, 10)
    f32 = jnp.float32
    x = jax.random.normal(ks[0], (BATCH, SEQ, D_MODEL), f32)
    norm1 = 1.0 + 0.01 * jax.random.normal(ks[1], (DEPTH, D_MODEL), f32)
    w_in = jax.random.normal(ks[2], (DEPTH, D_MODEL, N_IN), f32) * D_MODEL ** -0.5
    sinks = 0.5 * jax.random.normal(ks[3], (DEPTH, B_HEADS), f32)
    w_branch = jax.random.normal(ks[4], (DEPTH, N_BRANCH, BRANCH_WIDTH, D_MODEL), f32) * BRANCH_WIDTH ** -0.5
    w_out = jax.random.normal(ks[5], (DEPTH, D_MODEL, D_MODEL), f32) * D_MODEL ** -0.5
    norm2 = 1.0 + 0.01 * jax.random.normal(ks[6], (DEPTH, D_MODEL), f32)
    w_ff1 = jax.random.normal(ks[7], (DEPTH, D_MODEL, D_FF), f32) * D_MODEL ** -0.5
    w_ff2 = jax.random.normal(ks[8], (DEPTH, D_FF, D_MODEL), f32) * D_FF ** -0.5
    norm_f = 1.0 + 0.01 * jax.random.normal(ks[9], (D_MODEL,), f32)
    return {'x': x, 'norm1': norm1, 'w_in': w_in, 'sinks': sinks, 'w_branch': w_branch,
            'w_out': w_out, 'norm2': norm2, 'w_ff1': w_ff1, 'w_ff2': w_ff2, 'norm_f': norm_f}

def reference(x, norm1, w_in, sinks, w_branch, w_out, norm2, w_ff1, w_ff2, norm_f):
    cos, sin = rope_tables(x.shape[1], HEAD_DIM)
    for l in range(DEPTH):
        x = hybrid_layer(x, cos, sin, norm1[l], w_in[l], sinks[l], w_branch[l], w_out[l],
                         norm2[l], w_ff1[l], w_ff2[l])
    return rms_norm(x, norm_f)


_drawn_inputs = setup_inputs


def setup_inputs(seed=0):
    import zlib

    import numpy as np

    out = dict(_drawn_inputs(seed))
    spreads = {}
    factors = {'norm1': 3.817, 'sinks': 6.477, 'norm2': 4.346, 'norm_f': 5.637}
    for name, (base, spread) in spreads.items():
        noise = np.random.default_rng([zlib.crc32(name.encode()), seed]).standard_normal(out[name].shape)
        drawn = base * np.exp(spread * noise) if base else spread * noise
        out[name] = __import__('jax').numpy.asarray(drawn.astype(out[name].dtype))
    for name, factor in factors.items():
        out[name] = (out[name] * factor).astype(out[name].dtype)
    return out
```

```python
from contextlib import ExitStack

import concourse.bass as bass
from concourse import mybir

F32 = mybir.dt.float32
F32R = mybir.dt.float32r
BF16 = mybir.dt.bfloat16
ALU = mybir.AluOpType
ACT = mybir.ActivationFunctionType
AX = mybir.AxisListType

P = 128
SEQ = 256
MT = SEQ // P
D = 1024
KT = D // P
HD = 64
DFF = 4096
LAYERS = 2
EPS = 1e-6
QKV = 3268
GATES = 3 * D
N_IN = QKV + GATES
CW = 512
KU = 4
SHORT = QKV % CW
CHUNKS = 1 + N_IN // CW
QKV_CHUNKS = 1 + QKV // CW
RING = 4
RAW = 2
FFC = DFF // CW

K_STRAIGHT = 10
K_GATES = 2 * QKV_CHUNKS
K_BRANCH = K_GATES + 2 * (GATES // CW)
K_OUT = K_BRANCH + 6
K_UP0 = K_OUT + 4
K_LOOP = K_UP0 + 2
K_DOWN7 = K_LOOP + 4 * (FFC - 1)
UNITS = K_DOWN7 + 2
assert UNITS % RING == 0 and (K_LOOP - 2) % RING == 0

A_Q, A_K, A_V = 0, 512, 576
I_Q, I_K, I_W = 640, 896, 960
B_Q, B_K, B_V = 964, 1476, 1604
C_Q, C_K, C_V = 1732, 2244, 2756

SCALE = HD ** -0.5
IDX_SCALE = (64 ** -0.5) * (4 ** -0.5)
TOPK = SEQ // 4
ROUNDS = TOPK // 8
TAKEN = -3.0e38
MASKED = -1.0e30

STEPS = [("i", 0), ("i", 1)] + [(b, p) for b in "bca" for p in range(4)]
NS = len(STEPS)
Q_COL = {"a": A_Q, "i": I_Q, "b": B_Q, "c": C_Q}
BRANCHES = "bca"
BRANCH_INDEX = {"a": 0, "b": 1, "c": 2}
FIRST_A = STEPS.index(("a", 0))


def key_of(step):
    b, p = STEPS[step]
    if b == "i":
        return (I_K, 1) if p == 0 else None
    if b == "a":
        return (A_K, 1) if p == 0 else None
    if b == "b":
        return (B_K + HD * (p // 2), 1) if p % 2 == 0 else None
    return C_K + P * p, 2


KEY_JOB = {}
for _s in range(NS):
    KEY_JOB[_s] = (KEY_JOB[_s - 1] if _s else -1) + (key_of(_s) is not None)

T_JOBS = []
for _u in range(NS + 3):
    if _u < NS:
        T_JOBS.append(("q", _u))
        if key_of(_u):
            T_JOBS.append(("k", _u))
    if _u - 3 >= 2:
        T_JOBS.append(("o", _u - 3))
NT = len(T_JOBS)
NO = NS - 2


def value_col(branch, head):
    return {"a": A_V, "b": B_V + HD * (head // 4), "c": C_V + HD * head}[branch]


def program(nc, x, norm1, w_in, sinks, w_branch, w_out, norm2, w_ff1, w_ff2, norm_f, rope, masks,
            identity, out):
    win_v = w_in.rearrange("l (k p) n -> p (l k) n", p=P)
    wbr_v = w_branch.rearrange("l b (k p) n -> p (l b k) n", p=P)
    wout_v = w_out.rearrange("l (k p) n -> p (l k) n", p=P)
    wup_v = w_ff1.rearrange("l (k p) n -> p (l k) n", p=P)
    wdown_v = w_ff2.rearrange("l (k p) n -> p (l k) n", p=P)
    x_v = x.rearrange("b (m p) d -> p (b m) d", p=P)
    out_v = out.rearrange("b (m p) d -> p (b m) d", p=P)

    with ExitStack() as ctx:
        def sb(name, shape, dt=F32):
            return ctx.enter_context(nc.sbuf_tensor(name, shape, dt))

        def sem(name):
            return ctx.enter_context(nc.semaphore(name))

        bank = [ctx.enter_context(nc.psum_tensor(f"bank{i}", [P, 512], F32)) for i in range(8)]

        raw = sb("raw", [P, RAW, KU, CW])
        w_hi = sb("w_hi", [P, RING, KU, CW], F32R)
        w_lo = sb("w_lo", [P, RING, KU, CW], F32R)
        xs = sb("xs", [P, MT, D])
        h_hi = sb("h_hi", [P, KT, SEQ], F32R)
        h_lo = sb("h_lo", [P, KT, SEQ], F32R)
        br_hi = sb("br_hi", [P, 12, SEQ], F32R)
        br_lo = sb("br_lo", [P, 12, SEQ], F32R)
        act_hi = br_hi[:, 0:KU, :]
        act_lo = br_lo[:, 0:KU, :]
        proj = sb("proj", [P, MT, QKV])
        merged = proj[:, :, 0:D]
        gate = sb("gate", [P, MT, GATES])
        gate_flat = gate[:, :, :].rearrange("p m n -> p (m n)")
        rt1 = gate_flat[:, 0:1280]
        rt2 = gate_flat[:, 1280:2560]
        relu_dots = gate_flat[:, 2560:2560 + 4 * 384].rearrange("p (h n) -> p h n", h=4)
        score = gate_flat[:, 5632:6016]
        picked = gate_flat[:, 5120:5504]
        up_relu = gate_flat[:, 0:1024].rearrange("p (m n) -> p m n", m=MT)
        up_sq = gate_flat[:, 1024:2048].rearrange("p (m n) -> p m n", m=MT)
        squares = gate_flat[:, 2048:4096].rearrange("p (m n) -> p m n", m=MT)
        gain_f = gate_flat[:, 4096:5120]
        normed = gate_flat[:, 0:2048].rearrange("p (m n) -> p m n", m=MT)
        q_t = sb("q_t", [P, 2, SEQ])
        k_t = sb("k_t", [P, 2, SEQ])
        k_pair = sb("k_pair", [P, 4, MT, P])
        prob = sb("prob", [P, 2, 768])
        part = prob[:, :, :].rearrange("p a n -> p (a n)")[:, 0:1024].rearrange("p (m n) -> p m n", m=MT)
        prob_t = sb("prob_t", [P, 768])
        o_sb = sb("o_sb", [P, 2, 2, P])
        rope_sb = sb("rope_sb", [P, MT, 2, HD])
        mask_f = sb("mask_f", [P, 2, 384])
        mask_b = sb("mask_b", [P, 3, 384], BF16)
        causal_bias = sb("causal_bias", [P, 384])
        ident = sb("ident", [P, P])
        ident_neg = sb("ident_neg", [P, P], BF16)
        zeros = sb("zeros", [P, CW], BF16)
        top8 = sb("top8", [P, 2, 8])
        gain = sb("gain", [P, 2, KT])
        sink_neg = sb("sink_neg", [P, 8])
        sink_raw = sb("sink_raw", [P, 8])
        consts = sb("consts", [P, 4, 2])
        ssq = sb("ssq", [P, MT])
        var = sb("var", [P, 2, MT])
        rstd = sb("rstd", [P, MT])
        rstd_half = sb("rstd_half", [P, MT])
        row_max = sb("row_max", [P, 2, 4])
        neg_max = sb("neg_max", [P, 2, 4])
        row_sum = sb("row_sum", [P, 2, 4])
        sink_arg = sb("sink_arg", [P, 2, 4])
        sink_exp = sb("sink_exp", [P, 2, 4])
        row_inv = sb("row_inv", [P, 2, 4])

        raw_in = [sem(f"raw_in{i}") for i in range(RAW)]
        x_in, ident_in, const_in, small_in, out_sent, gf_in = (sem(n) for n in (
            "x_in", "ident_in", "const_in", "small_in", "out_sent", "gf_in"))
        hi_ready = sem("hi_ready")
        lo_ready = sem("lo_ready")
        mm_done = sem("mm_done")
        x_ready = sem("x_ready")
        const_ready = sem("const_ready")
        zero_ready = sem("zero_ready")
        half_t = sem("half_t")
        half_hi = sem("half_hi")
        half_lo = sem("half_lo")
        ssq_ready = sem("ssq_ready")
        rstd_ready = sem("rstd_ready")
        proj_ready = sem("proj_ready")
        rope_done = sem("rope_done")
        t_done = sem("t_done")
        t_taken = sem("t_taken")
        ot_lo = sem("ot_lo")
        s_done = sem("s_done")
        neg_ready = sem("neg_ready")
        exp_done = sem("exp_done")
        sink_arg_ready = sem("sink_arg_ready")
        sink_exp_ready = sem("sink_exp_ready")
        pt_done = sem("pt_done")
        pt1_taken = sem("pt1_taken")
        pt0_taken = sem("pt0_taken")
        pv_done = sem("pv_done")
        o_ready = sem("o_ready")
        chosen = sem("chosen")
        part_ready = sem("part_ready")
        part_added = sem("part_added")
        relu_ready = sem("relu_ready")
        sq_ready = sem("sq_ready")
        act_t = sem("act_t")
        act_t_hi = sem("act_t_hi")
        act_t_lo = sem("act_t_lo")
        dve_step = sem("dve_step")
        pool_step = sem("pool_step")
        y_ready = sem("y_ready")
        wait_passed = sem("wait_passed")

        def proj_no(l, n):
            return l * (2 * CHUNKS) + (n + 1)

        def unit_no(l, k, it=None):
            n = l * UNITS + k
            return n if it is None else n + it * RING

        def half_no(l, k, m, it=None):
            n = l * (2 * UNITS) + (2 * k + m + 1 + 2 * RING)
            return n if it is None else n + it * (2 * RING)

        class Count:
            def __init__(self, per_layer):
                self.per_layer, self.n = per_layer, 0

            def one_more(self):
                self.n += 1
                return 1

            def value(self, l, n=None):
                return l * self.per_layer + (self.n if n is None else n)

        DVE_PER_LAYER = 1 + 2 * 4 + 1 + 4 * ROUNDS + 4 * NO + 4 + NO
        POOL_PER_LAYER = 2 * 3 + 5

        block = ctx.enter_context(nc.Block())

        @block.sync
        def _(sp):
            sp.sem_inc(lo_ready, RAW)
            sp.dma_start(xs[:, :, :], x_v).then_inc(x_in, 16)

            def load(l, k, source, it=None, width=CW):
                sp.wait_ge(lo_ready, unit_no(l, k, it) + 1)
                sp.dma_start(raw[:, k % RAW, :, 0:width], source).then_inc(raw_in[k % RAW], 16)

            with sp.Fori(0, LAYERS) as l:
                sp.wait_ge(lo_ready, unit_no(l, 0) + 1)
                sp.dma_start(gain[:, 0, :], norm1[:, bass.ds(l * KT, KT)]).then_inc(small_in, 16)
                sp.dma_start(gain[:, 1, :], norm2[:, bass.ds(l * KT, KT)]).then_inc(small_in, 16)
                sp.dma_start(sink_raw[:, :], sinks[bass.ds(l, 1), :].to_broadcast([P, 8])).then_inc(small_in, 16)
                for r in range(2):
                    load(l, r, win_v[:, bass.ds(l * KT + r * KU, KU), 0:SHORT], width=SHORT)
                with sp.Fori(0, (K_BRANCH - 2) // RING) as i:
                    for j in range(RING):
                        col = i * (2 * CW) + (SHORT + (j // 2) * CW)
                        load(l, 2 + j, win_v[:, bass.ds(l * KT + (j % 2) * KU, KU), bass.ds(col, CW)], it=i)
                for r in range(6):
                    c, b = r // 3, BRANCH_INDEX[BRANCHES[r % 3]]
                    load(l, K_BRANCH + r, wbr_v[:, bass.ds(l * 12 + b * KU, KU), c * CW:(c + 1) * CW])
                for r in range(4):
                    load(l, K_OUT + r, wout_v[:, bass.ds(l * KT + (r // 2) * KU, KU),
                                              (r % 2) * CW:(r % 2 + 1) * CW])
                for r in range(2):
                    load(l, K_UP0 + r, wup_v[:, bass.ds(l * KT + r * KU, KU), 0:CW])
                with sp.Fori(0, FFC - 1) as i:
                    for r in range(2):
                        load(l, K_LOOP + r, wup_v[:, bass.ds(l * KT + r * KU, KU), bass.ds((i + 1) * CW, CW)],
                             it=i)
                    for r in range(2):
                        load(l, K_LOOP + 2 + r, wdown_v[:, bass.ds(l * (DFF // P) + i * KU, KU),
                                                        r * CW:(r + 1) * CW], it=i)
                for r in range(2):
                    load(l, K_DOWN7 + r, wdown_v[:, bass.ds(l * (DFF // P) + (FFC - 1) * KU, KU),
                                                 r * CW:(r + 1) * CW])
            sp.wait_ge(act_t, 2 * FFC * LAYERS)
            sp.dma_start(gain_f, norm_f.rearrange("(o n) -> o n", o=1).to_broadcast([P, D])).then_inc(gf_in, 16)
            for m in range(MT):
                sp.wait_ge(y_ready, m + 1)
                sp.dma_start(out_v[:, m, :], normed[:, m, :]).then_inc(out_sent, 16)
            sp.wait_ge(out_sent, 16 * MT)

        @block.scalar
        def _(act):
            act.sem_inc(proj_ready, 1)
            act.dma_start(ident[:, :], identity).then_inc(ident_in, 16)
            act.dma_start(rope_sb[:, :, :, :], rope).then_inc(const_in, 16)
            act.dma_start(mask_f[:, :, :], masks).then_inc(const_in, 16)

            def high(l, k, it=None, width=CW):
                n = l * (UNITS // RAW) + (k // RAW + 1)
                if it is not None:
                    n = n + it * (RING // RAW)
                act.wait_ge(raw_in[k % RAW], n * 16)
                act.wait_ge(mm_done, half_no(l, k - RING, 1, it))
                act.activation(w_hi[:, k % RING, :, 0:width], raw[:, k % RAW, :, 0:width],
                               ACT.Copy).then_inc(hi_ready, 1)

            def half_high(l, group, c, gains):
                for b in range(2):
                    act.wait_ge(half_t, l * 12 + (4 * group + 2 * c + b + 1))
                    src = bank[(6, 4)[c] + b]
                    kt = 4 * c + 2 * b
                    if gains is None:
                        act.activation(h_hi[:, kt:kt + 2, :], src[:, :].rearrange("p (a n) -> p a n", a=2),
                                       ACT.Copy, scale=0.5).then_inc(half_hi, 1)
                    else:
                        act.activation(h_hi[:, kt, :], src[:, 0:SEQ], ACT.Identity, bias=0.0,
                                       scale=gain[:, gains, kt:kt + 1])
                        act.activation(h_hi[:, kt + 1, :], src[:, SEQ:512], ACT.Identity, bias=0.0,
                                       scale=gain[:, gains, kt + 1:kt + 2]).then_inc(half_hi, 1)

            def sum_squares(l, which):
                act.wait_ge(x_ready, l * 8 + 4 * (which + 1))
                for m in range(MT):
                    act.activation(squares[:, m, :], xs[:, m, :], ACT.Square,
                                   accum_out=ssq[:, m:m + 1]).then_inc(ssq_ready, 1)

            def take_proj(l, e, k, m, it=None):
                act.wait_ge(mm_done, half_no(l, k, m, it))
                src = bank[(2 * (e % 2) if e < 5 else 0) + m]
                if e < QKV_CHUNKS:
                    if e == 0:
                        dst, src = proj[:, m, 0:SHORT], src[:, 0:SHORT]
                    else:
                        lo = SHORT + (e - 1) * CW
                        dst = proj[:, m, lo:lo + CW]
                        src = src[:, :]
                    act.activation(dst, src, ACT.Identity, bias=0.0,
                                   scale=rstd[:, m:m + 1]).then_inc(proj_ready, 1)
                else:
                    g = e - QKV_CHUNKS
                    act.activation(gate[:, m, g * CW:(g + 1) * CW], src[:, :], ACT.Tanh, bias=0.0,
                                   scale=rstd_half[:, m:m + 1]).then_inc(proj_ready, 1)

            def take_t(l, kind, step):
                j = T_JOBS.index((kind, step))
                act.wait_ge(t_done, l * NT + j + 1)
                src = bank[6][:, 0:SEQ]
                if kind == "q":
                    act.activation(q_t[:, step % 2, :], src, ACT.Copy).then_inc(t_taken, 1)
                elif kind == "k":
                    act.activation(k_t[:, KEY_JOB[step] % 2, :], src, ACT.Copy).then_inc(t_taken, 1)
                else:
                    b, p = STEPS[step]
                    act.activation(br_hi[:, 4 * BRANCH_INDEX[b] + p, :], src, ACT.Copy).then_inc(t_taken, 1)

            def exponentials(l, s):
                par = s % 2
                act.wait_ge(s_done, l * 2 * NS + 2 * s + 2)
                if s < 2:
                    for j in range(2):
                        act.activation(relu_dots[:, 2 * s + j, :], bank[2 + j][:, 0:384],
                                       ACT.Relu).then_inc(exp_done, 2)
                    return
                act.wait_ge(neg_ready, l * NO + (s - 2) + 1)
                for n in range(4):
                    lo, w = (0, 256) if n < 2 else (256, 128)
                    act.activation(prob[:, par, 384 * (n % 2) + lo:384 * (n % 2) + lo + w],
                                   bank[2 + n % 2][:, lo:lo + w], ACT.Exp, bias=neg_max[:, par, n:n + 1],
                                   scale=SCALE, accum_out=row_sum[:, par, n:n + 1]).then_inc(exp_done, 1)
                if STEPS[s][0] == "b":
                    act.wait_ge(sink_arg_ready, l * 4 + (s - 2) + 1)
                    act.activation(sink_exp[:, par, :], sink_arg[:, par, :], ACT.Exp).then_inc(sink_exp_ready, 1)

            def take_probs(l, s):
                act.wait_ge(pt_done, l * 2 * NO + 2 * (s - 2) + 1)
                act.activation(prob_t[:, 0:512], bank[4][:, :], ACT.Copy).then_inc(pt1_taken, 1)

            def hidden_high(l, it):
                for b in range(2):
                    act.wait_ge(act_t, l * 2 * FFC + it * 2 + b + 1)
                    act.activation(act_hi[:, 2 * b:2 * b + 2, :],
                                   bank[6 + b][:, :].rearrange("p (a n) -> p a n", a=2),
                                   ACT.Copy).then_inc(act_t_hi, 1)

            def take_up(l, k, it, chunk):
                for m in range(MT):
                    act.wait_ge(mm_done, half_no(l, k + 1, m, it))
                    if it is not None:
                        act.wait_ge(sq_ready, l * 2 * FFC + chunk * 2)
                    act.activation(up_relu[:, m, :], bank[m][:, :], ACT.Relu,
                                   scale=rstd[:, m:m + 1]).then_inc(relu_ready, 1)

            with act.Fori(0, LAYERS) as l:
                for k in range(2):
                    high(l, k, width=SHORT)
                act.wait_ge(small_in, l * 48 + 48)
                half_high(l, 0, 0, 0)
                half_high(l, 0, 1, 0)
                sum_squares(l, 0)
                high(l, 2)
                high(l, 3)
                act.wait_ge(rstd_ready, l * 2 + 1)
                for m in range(MT):
                    take_proj(l, 0, 1, m)
                with act.Fori(0, 2) as i:
                    for j in range(2):
                        high(l, 4 + 2 * j, it=i)
                        high(l, 5 + 2 * j, it=i)
                        for m in range(MT):
                            act.wait_ge(mm_done, half_no(l, 3 + 2 * j, m, i))
                            act.activation(proj[:, m, bass.ds(i * (2 * CW) + (SHORT + j * CW), CW)],
                                           bank[2 * (1 - j) + m][:, :], ACT.Identity, bias=0.0,
                                           scale=rstd[:, m:m + 1]).then_inc(proj_ready, 1)
                for u in range(K_OUT - K_STRAIGHT):
                    k = K_STRAIGHT + u
                    high(l, k + 2)
                    if u < NS:
                        take_t(l, "q", u)
                    if 1 <= u <= NS:
                        exponentials(l, u - 1)
                    if 4 <= u <= NS + 1:
                        take_probs(l, u - 2)
                    last = k < K_BRANCH and k % 2 == 1
                    e = k // 2
                    if k == K_GATES + 1:
                        act.wait_ge(rope_done, l * 5 + 5)
                        act.wait_ge(chosen, l * 2 + 1)
                    if k == K_GATES + 9:
                        act.wait_ge(chosen, l * 2 + 2)
                    if last:
                        take_proj(l, e, k, 0)
                    if u < NS and key_of(u):
                        take_t(l, "k", u)
                    if last:
                        take_proj(l, e, k, 1)
                    if 5 <= u <= NS + 2:
                        take_t(l, "o", u - 3)
                    if k == K_BRANCH + 4:
                        half_high(l, 1, 0, None)
                high(l, K_OUT + 2)
                high(l, K_OUT + 3)
                half_high(l, 1, 1, None)
                high(l, K_OUT + 4)
                half_high(l, 2, 0, 1)
                high(l, K_OUT + 5)
                half_high(l, 2, 1, 1)
                sum_squares(l, 1)
                high(l, K_LOOP)
                high(l, K_LOOP + 1)
                act.wait_ge(rstd_ready, l * 2 + 2)
                take_up(l, K_UP0, None, 0)
                hidden_high(l, 0)
                with act.Fori(0, FFC - 1) as i:
                    high(l, K_LOOP + 2, it=i)
                    high(l, K_LOOP + 3, it=i)
                    take_up(l, K_LOOP, i, i + 1)
                    high(l, K_LOOP + 4, it=i)
                    high(l, K_LOOP + 5, it=i)
                    hidden_high(l, i + 1)
            sum_squares(LAYERS - 1, 2)

        @block.vector
        def _(dve):
            dve.memset(zeros[:, :], 0.0).then_inc(zero_ready, 1)
            dve.memset(consts[:, 0, :], 1.0 / D).then_inc(zero_ready, 1)
            dve.memset(consts[:, 1, :], EPS).then_inc(zero_ready, 1)
            dve.memset(consts[:, 2, :], -0.5).then_inc(zero_ready, 1)
            dve.memset(consts[:, 3, :], 0.5).then_inc(zero_ready, 1)
            dve.wait_ge(x_in, 16)
            dve.sem_inc(x_ready, 4)
            dve.wait_ge(ident_in, 16)
            dve.tensor_scalar(ident_neg[:, :], ident[:, :], MASKED, None, ALU.mult).then_inc(const_ready, 1)
            dve.wait_ge(const_in, 32)
            dve.tensor_copy(mask_b[:, 0:2, :], mask_f[:, :, :]).then_inc(const_ready, 1)
            dve.tensor_scalar(causal_bias[:, :], mask_f[:, 0, :], MASKED, None, ALU.mult).then_inc(const_ready, 1)
            dve.wait_ge(const_ready, 3)

            def low(l, k, it=None, width=CW):
                dve.wait_ge(hi_ready, unit_no(l, k, it) + 1)
                dve.tensor_tensor(w_lo[:, k % RING, :, 0:width], raw[:, k % RAW, :, 0:width],
                                  w_hi[:, k % RING, :, 0:width].bitcast(F32),
                                  ALU.subtract).then_inc(lo_ready, 1)

            def half_low(l, group, c, gains):
                for b in range(2):
                    dve.wait_ge(half_hi, l * 12 + (4 * group + 2 * c + b + 1))
                    src = bank[(6, 4)[c] + b]
                    kt = 4 * c + 2 * b
                    if gains is None:
                        dve.scalar_tensor_tensor(
                            h_lo[:, kt:kt + 2, :], src[:, :].rearrange("p (a n) -> p a n", a=2), 0.5,
                            h_hi[:, kt:kt + 2, :].bitcast(F32), ALU.mult, ALU.subtract).then_inc(half_lo, 1)
                        continue
                    for a in range(2):
                        ins = dve.scalar_tensor_tensor(
                            h_lo[:, kt + a, :], src[:, a * SEQ:(a + 1) * SEQ], gain[:, gains, kt + a:kt + a + 1],
                            h_hi[:, kt + a, :].bitcast(F32), ALU.mult, ALU.subtract)
                    ins.then_inc(half_lo, 1)

            def add_to_x(l, c, k, banks, count=None):
                for m in range(MT):
                    dve.wait_ge(mm_done, half_no(l, k, m))
                    cols = xs[:, m, c * CW:(c + 1) * CW]
                    dve.tensor_tensor(cols, cols, bank[banks + m][:, :], ALU.add).then_inc(x_ready, 1)

            def maxima(l, own, s):
                par, b = s % 2, STEPS[s][0]
                dve.wait_ge(s_done, l * 2 * NS + 2 * s + 2)
                for n in range(4):
                    lo, w = (0, 256) if n < 2 else (256, 128)
                    dve.tensor_reduce(row_max[:, par, n:n + 1], bank[2 + n % 2][:, lo:lo + w],
                                      AX.X, ALU.max).then_inc(dve_step, own.one_more())
                dve.wait_ge(dve_step, own.value(l))
                if b != "b":
                    dve.tensor_scalar(neg_max[:, par, :], row_max[:, par, :], -SCALE, None,
                                      ALU.mult).then_inc(neg_ready, 1)
                    return
                p = STEPS[s][1]
                sk = sink_neg[:, 2 * p:2 * p + 2].unsqueeze(1).to_broadcast([P, 2, 2])
                dve.scalar_tensor_tensor(
                    neg_max[:, par, :].rearrange("p (m h) -> p m h", m=2),
                    row_max[:, par, :].rearrange("p (m h) -> p m h", m=2), -SCALE, sk,
                    ALU.mult, ALU.min).then_inc(neg_ready, 1)
                dve.wait_ge(neg_ready, l * NO + (s - 2) + 1)
                dve.tensor_tensor(sink_arg[:, par, :].rearrange("p (m h) -> p m h", m=2),
                                  neg_max[:, par, :].rearrange("p (m h) -> p m h", m=2), sk,
                                  ALU.subtract).then_inc(sink_arg_ready, 1)

            def take_probs(l, s):
                dve.wait_ge(pt_done, l * 2 * NO + 2 * (s - 2) + 2)
                dve.tensor_copy(prob_t[:, 512:768], bank[5][:, 0:256]).then_inc(pt0_taken, 1)

            def inverse_sums(l, own, s):
                par = s % 2
                dve.wait_ge(exp_done, l * 4 * NS + 4 * s + 4)
                if STEPS[s][0] == "b":
                    dve.wait_ge(sink_exp_ready, l * 4 + (s - 2) + 1)
                    dve.tensor_tensor(row_sum[:, par, :], row_sum[:, par, :], sink_exp[:, par, :],
                                      ALU.add).then_inc(dve_step, own.one_more())
                    dve.wait_ge(dve_step, own.value(l))
                dve.reciprocal(row_inv[:, par, :], row_sum[:, par, :]).then_inc(dve_step, own.one_more())
                return own.n

            def normalise(l, own, s, n):
                par = s % 2
                dve.wait_ge(pv_done, l * NO + (s - 2) + 1)
                dve.wait_ge(dve_step, own.value(l, n))
                dve.tensor_tensor(
                    o_sb[:, par, :, :].rearrange("p m (h d) -> p (m h) d", h=2),
                    bank[7][:, 0:256].rearrange("p (a d) -> p a d", a=4),
                    row_inv[:, par, :].unsqueeze(2).to_broadcast([P, 4, HD]), ALU.mult).then_inc(o_ready, 1)

            def out_low(l, s):
                b, p = STEPS[s]
                j = T_JOBS.index(("o", s))
                dve.wait_ge(t_taken, l * NT + j + 1)
                kt = 4 * BRANCH_INDEX[b] + p
                dve.tensor_tensor(br_lo[:, kt, :], bank[6][:, 0:SEQ], br_hi[:, kt, :].bitcast(F32),
                                  ALU.subtract).then_inc(ot_lo, 1)

            def index_scores(l, own, s):
                dve.wait_ge(exp_done, l * 4 * NS + 4 * s + 4)
                for j in range(2):
                    h = 2 * s + j
                    for m, lo, w in ((1, 0, 256), (0, 256, 128)):
                        cols = score[:, lo:lo + w]
                        wt = proj[:, m, I_W + h:I_W + h + 1]
                        if h == 0:
                            dve.tensor_scalar(cols, relu_dots[:, h, lo:lo + w], wt, None,
                                              ALU.mult).then_inc(dve_step, own.one_more())
                        else:
                            dve.wait_ge(dve_step, own.value(l, own.n - 1))
                            dve.scalar_tensor_tensor(cols, relu_dots[:, h, lo:lo + w], wt, cols, ALU.mult,
                                                     ALU.add).then_inc(dve_step, own.one_more())

            def settled(l, own):
                dve.wait_ge(dve_step, own.value(l))
                dve.sem_inc(wait_passed, 1)

            def top_round(l, own):
                spans = ((0, 0, 256), (1, 256, 128))
                settled(l, own)
                for m, lo, w in spans:
                    dve.max(top8[:, m, :], picked[:, lo:lo + w]).then_inc(dve_step, own.one_more())
                settled(l, own)
                for m, lo, w in spans:
                    dve.match_replace(picked[:, lo:lo + w], top8[:, m, :], picked[:, lo:lo + w],
                                      TAKEN).then_inc(dve_step, own.one_more())

            with dve.Fori(0, LAYERS) as l:
                own = Count(DVE_PER_LAYER)
                low(l, 0, width=SHORT)
                dve.wait_ge(small_in, l * 48 + 48)
                half_low(l, 0, 0, 0)
                low(l, 1, width=SHORT)
                half_low(l, 0, 1, 0)
                dve.tensor_scalar(sink_neg[:, :], sink_raw[:, :], -1.0, None,
                                  ALU.mult).then_inc(dve_step, own.one_more())
                low(l, 2)
                low(l, 3)
                with dve.Fori(0, 2) as i:
                    for j in range(RING):
                        low(l, 4 + j, it=i)
                inverse = {}
                for u in range(K_OUT - K_STRAIGHT):
                    k = K_STRAIGHT + u
                    if 3 <= u <= NS:
                        maxima(l, own, u - 1)
                    low(l, k + 2)
                    if 1 <= u <= 2:
                        index_scores(l, own, u - 1)
                    if u == 2:
                        dve.wait_ge(dve_step, own.value(l))
                        dve.scalar_tensor_tensor(picked[:, :], score[:, :], IDX_SCALE, causal_bias[:, :],
                                                 ALU.mult, ALU.add).then_inc(dve_step, own.one_more())
                        dve.wait_ge(dve_step, own.value(l))
                        dve.sem_inc(chosen, 1)
                    if 4 <= u <= NS + 1:
                        take_probs(l, u - 2)
                        inverse[u - 2] = inverse_sums(l, own, u - 2)
                    if 3 <= u < 3 + ROUNDS:
                        top_round(l, own)
                    if u == FIRST_A:
                        dve.wait_ge(dve_step, own.value(l))
                        dve.scalar_tensor_tensor(mask_b[:, 2, :], picked[:, :], TAKEN, mask_f[:, 0, :],
                                                 ALU.is_gt, ALU.add).then_inc(chosen, 1)
                    if 4 <= u <= NS + 1:
                        normalise(l, own, u - 2, inverse[u - 2])
                    if 5 <= u <= NS + 2:
                        out_low(l, u - 3)
                    if k >= K_BRANCH:
                        r = k - K_BRANCH
                        c, b = r // 3, BRANCH_INDEX[BRANCHES[r % 3]]
                        for m in range(MT):
                            dve.wait_ge(mm_done, half_no(l, k, m))
                            dve.wait_ge(proj_ready, proj_no(l, 2 * CHUNKS))
                            dst = merged[:, m, c * CW:(c + 1) * CW] if r % 3 == 0 else part[:, m, :]
                            if r % 3:
                                prior = 2 * (2 * c + r % 3 - 1) - 2 + m + 1
                                if prior > 0:
                                    dve.wait_ge(part_added, l * 8 + prior)
                            dve.scalar_tensor_tensor(dst, gate[:, m, b * D + c * CW:b * D + (c + 1) * CW], 1.0,
                                                     bank[2 * (r % 2) + m][:, :], ALU.add,
                                                     ALU.mult).then_inc(part_ready, 1)
                    if k == K_BRANCH + 4:
                        half_low(l, 1, 0, None)
                assert own.n == DVE_PER_LAYER, (own.n, DVE_PER_LAYER)
                low(l, K_OUT + 2)
                low(l, K_OUT + 3)
                half_low(l, 1, 1, None)
                low(l, K_OUT + 4)
                add_to_x(l, 0, K_OUT + 2, 0)
                half_low(l, 2, 0, 1)
                low(l, K_OUT + 5)
                add_to_x(l, 1, K_OUT + 3, 2)
                half_low(l, 2, 1, 1)
                low(l, K_LOOP)
                low(l, K_LOOP + 1)

                def hidden_low(chunk):
                    for b in range(2):
                        dve.wait_ge(act_t_hi, l * 2 * FFC + chunk * 2 + b + 1)
                        dve.tensor_tensor(act_lo[:, 2 * b:2 * b + 2, :],
                                          bank[6 + b][:, :].rearrange("p (a n) -> p a n", a=2),
                                          act_hi[:, 2 * b:2 * b + 2, :].bitcast(F32),
                                          ALU.subtract).then_inc(act_t_lo, 1)

                hidden_low(0)
                with dve.Fori(0, FFC - 1) as i:
                    for j in range(RING):
                        low(l, K_LOOP + 2 + j, it=i)
                    hidden_low(i + 1)
                add_to_x(l, 0, K_DOWN7, 2)
                add_to_x(l, 1, K_DOWN7 + 1, 4)
            dve.wait_ge(rstd_ready, 2 * LAYERS + 1)
            dve.wait_ge(gf_in, 16)
            for m in range(MT):
                dve.scalar_tensor_tensor(normed[:, m, :], xs[:, m, :], rstd[:, m:m + 1], gain_f,
                                         ALU.mult, ALU.mult).then_inc(y_ready, 1)

        @block.gpsimd
        def _(pool):
            pool.wait_ge(zero_ready, 5)
            pool.wait_ge(const_in, 32)

            def inverse_rms(count, done):
                pool.wait_ge(ssq_ready, count * 2)
                pool.tensor_tensor(var[:, 0, :], ssq[:, :], consts[:, 0, :], ALU.mult).then_inc(pool_step, 1)
                pool.wait_ge(pool_step, done(1))
                pool.tensor_tensor(var[:, 1, :], var[:, 0, :], consts[:, 1, :], ALU.add).then_inc(pool_step, 1)
                pool.wait_ge(pool_step, done(2))
                pool.tensor_tensor(rstd[:, :], var[:, 1, :], consts[:, 2, :], ALU.pow).then_inc(pool_step, 1)
                pool.wait_ge(pool_step, done(3))
                pool.tensor_tensor(rstd_half[:, :], rstd[:, :], consts[:, 3, :], ALU.mult).then_inc(rstd_ready, 1)

            sections = ((A_Q, 9, 2, ((8, 0),)), (I_Q, 5, 3, ((4, 1),)), (B_Q, 10, 4, ((8, 2), (9, 3))),
                        (C_Q, 8, 5, ()), (C_K, 8, 6, ()))
            with pool.Fori(0, LAYERS) as l:
                inverse_rms(l * 2 + 1, lambda n: l * POOL_PER_LAYER + n)
                for n, (col, heads, chunks, shared) in enumerate(sections):
                    if n:
                        pool.wait_ge(rope_done, l * 5 + n)
                    pool.wait_ge(proj_ready, proj_no(l, 2 * chunks))
                    v = proj[:, :, col:col + heads * HD].rearrange("p m (h d) -> p m h d", d=HD)
                    t1 = rt1[:, 0:2 * heads * HD].rearrange("p (m h d) -> p m h d", m=MT, d=HD)
                    t2 = rt2[:, 0:2 * heads * HD].rearrange("p (m h d) -> p m h d", m=MT, d=HD)
                    cs = rope_sb[:, :, 0, :].unsqueeze(2).to_broadcast([P, MT, heads, HD])
                    sn = rope_sb[:, :, 1, :].unsqueeze(2)
                    half = HD // 2
                    pool.tensor_tensor(t1, v, cs, ALU.mult)
                    pool.tensor_tensor(t2[:, :, :, 0:half], v[:, :, :, half:HD],
                                       sn[:, :, :, 0:half].to_broadcast([P, MT, heads, half]), ALU.mult)
                    pool.tensor_tensor(t2[:, :, :, half:HD], v[:, :, :, 0:half],
                                       sn[:, :, :, half:HD].to_broadcast([P, MT, heads, half]),
                                       ALU.mult).then_inc(pool_step, 1)
                    pool.wait_ge(pool_step, l * POOL_PER_LAYER + (3 + n + 1))
                    for h, place in shared:
                        two = [P, MT, 2, HD]
                        pool.tensor_tensor(k_pair[:, place, :, :].rearrange("p m (t d) -> p m t d", t=2),
                                           t1[:, :, h, :].unsqueeze(2).to_broadcast(two),
                                           t2[:, :, h, :].unsqueeze(2).to_broadcast(two), ALU.add)
                    pool.tensor_tensor(v, t1, t2, ALU.add).then_inc(rope_done, 1)
                for r in range(6):
                    if r % 3 == 0:
                        continue
                    c = r // 3
                    for m in range(MT):
                        pool.wait_ge(part_ready, l * 12 + 2 * r + m + 1)
                        if r % 3 == 2:
                            pool.wait_ge(part_added, l * 8 + 4 * c + m + 1)
                        cols = merged[:, m, c * CW:(c + 1) * CW]
                        pool.tensor_tensor(cols, cols, part[:, m, :], ALU.add).then_inc(part_added, 1)
                inverse_rms(l * 2 + 2, lambda n: l * POOL_PER_LAYER + (8 + n))

                def square(chunk, first=False):
                    for m in range(MT):
                        pool.wait_ge(relu_ready, l * 2 * FFC + chunk * 2 + m + 1)
                        if not first:
                            pool.wait_ge(act_t, l * 2 * FFC + chunk * 2)
                        pool.tensor_tensor(up_sq[:, m, :], up_relu[:, m, :], up_relu[:, m, :],
                                           ALU.mult).then_inc(sq_ready, 1)

                square(0, first=True)
                with pool.Fori(0, FFC - 1) as i:
                    square(i + 1)
            inverse_rms(2 * LAYERS + 1, lambda n: LAYERS * POOL_PER_LAYER + n)

        @block.tensor
        def _(pe):
            pe.wait_ge(ident_in, 16)
            pe.sem_inc(mm_done, 2 * RING)

            def unit(l, k, left_hi, left_lo, banks, first, last, it=None, width=CW, free=None, pauses=None,
                     start_flag=None):
                slot, n = k % RING, 0
                pe.wait_ge(lo_ready, unit_no(l, k, it) + 1 + RAW)
                for m in range(MT):
                    if free:
                        free(m)
                    for kt in range(KU):
                        rows = slice(m * P, (m + 1) * P)
                        for p, (a, w) in enumerate(((left_hi, w_hi), (left_hi, w_lo), (left_lo, w_hi))):
                            if pauses and n % 4 == 0 and n // 4 in pauses:
                                pauses[n // 4]()
                            n += 1
                            ins = pe.matmul(bank[banks + m][:, 0:width], a[:, kt, rows],
                                            w[:, slot, kt, 0:width],
                                            start=first and kt == 0 and p == 0,
                                            stop=last and kt == KU - 1 and p == 2)
                    ins.then_inc(mm_done, 1)

            def rows_of(t, n):
                return t[:, KU * n:KU * (n + 1), :]

            def transpose_half(l, group, c, src):
                for b in range(2):
                    for a in range(2):
                        for m in range(MT):
                            kt = 4 * c + 2 * b + a
                            ins = pe.transpose(bank[(6, 4)[c] + b][:, a * SEQ + m * P:a * SEQ + (m + 1) * P],
                                               src[:, m, kt * P:(kt + 1) * P], ident[:, :])
                    ins.then_inc(half_t, 1)

            def t_job(l, kind, step):
                j = T_JOBS.index((kind, step))
                before = sum(1 for x in T_JOBS[:j] if x[0] == "o")
                b, p = STEPS[step]
                if j:
                    pe.wait_ge(t_taken, l * NT + j)
                if before:
                    pe.wait_ge(ot_lo, l * NO + before)
                if kind == "o":
                    pe.wait_ge(o_ready, l * NO + (step - 2) + 1)
                else:
                    pe.wait_ge(rope_done, l * 5 + {"i": 2, "b": 3, "c": 5, "a": 5}[b])
                for m in range(MT):
                    if kind == "q":
                        src = proj[:, m, Q_COL[b] + P * p:Q_COL[b] + P * (p + 1)]
                    elif kind == "o":
                        src = o_sb[:, step % 2, 1 - m, :]
                    else:
                        col, heads = key_of(step)
                        if heads == 2:
                            src = proj[:, m, col:col + P]
                        else:
                            src = k_pair[:, {A_K: 0, I_K: 1, B_K: 2, B_K + HD: 3}[col], m, :]
                    ins = pe.transpose(bank[6][:, m * P:(m + 1) * P], src, ident[:, :])
                ins.then_inc(t_done, 1)

            def scores(l, s):
                b, p = STEPS[s]
                q_job = T_JOBS.index(("q", s))
                jobs = [q_job] + [T_JOBS.index(("k", x)) for x in range(s + 1) if key_of(x)][-1:]
                pe.wait_ge(t_taken, l * NT + max(jobs) + 1)
                if s:
                    pe.wait_ge(exp_done, l * 4 * NS + 4 * s)
                if s == FIRST_A:
                    pe.wait_ge(chosen, l * 2 + 2)
                kb = k_t[:, KEY_JOB[s] % 2, :]
                if b != "i":
                    if s == 2:
                        pe.wait_ge(const_ready, 3)
                    for j in range(2):
                        pe.matmul(bank[2 + j][:, 0:384], ident_neg[:, :],
                                  mask_b[:, {"c": 0, "b": 1, "a": 2}[b], :], start=True, stop=False)
                for m, keys, lo in ((1, 256, 0), (0, 128, 256)):
                    for j in range(2):
                        rows = slice(HD * j, HD * j + HD)
                        ins = pe.matmul(bank[2 + j][:, lo:lo + keys],
                                        q_t[rows, s % 2, m * P:(m + 1) * P], kb[rows, 0:keys],
                                        start=b == "i", stop=b == "i" or m == 0)
                        if m == 0:
                            ins.then_inc(s_done, 1)

            def transpose_probs(l, s):
                par = s % 2
                pe.wait_ge(exp_done, l * 4 * NS + 4 * s + 4)
                if s > 2:
                    pe.wait_ge(pt1_taken, l * NO + s - 2)
                    pe.wait_ge(pt0_taken, l * NO + s - 2)
                for n in range(6):
                    dst = bank[4][:, n * P:(n + 1) * P] if n < 4 else bank[5][:, (n - 4) * P:(n - 3) * P]
                    ins = pe.transpose(dst, prob[:, par, n * P:(n + 1) * P], ident[:, :])
                    if n in (3, 5):
                        ins.then_inc(pt_done, 1)

            def values(l, s):
                b, p = STEPS[s]
                pe.wait_ge(pt1_taken, l * NO + s - 1)
                pe.wait_ge(pt0_taken, l * NO + s - 1)
                if b == "c":
                    pe.wait_ge(proj_ready, proj_no(l, 2 * QKV_CHUNKS))
                if s > 2:
                    pe.wait_ge(o_ready, l * NO + s - 2)
                for n in range(4):
                    col = value_col(b, 2 * p + n % 2)
                    blocks = 2 if n < 2 else 1
                    for kb in range(blocks):
                        at = 3 * (n % 2) + (kb if n < 2 else 2)
                        ins = pe.matmul(bank[7][:, n * HD:(n + 1) * HD], prob_t[:, at * P:(at + 1) * P],
                                        proj[:, kb, col:col + HD], start=kb == 0, stop=kb == blocks - 1)
                ins.then_inc(pv_done, 1)

            with pe.Fori(0, LAYERS) as l:
                pe.wait_ge(x_ready, l * 8 + 2)
                transpose_half(l, 0, 0, xs)
                for r in range(2):
                    pauses = {}
                    if r == 0:
                        def x_half():
                            pe.wait_ge(x_ready, l * 8 + 4)
                            transpose_half(l, 0, 1, xs)
                        pauses[4] = x_half
                    pe.wait_ge(half_lo, l * 12 + 2 * r + 2)
                    unit(l, r, rows_of(h_hi, r), rows_of(h_lo, r), 0, r == 0, r == 1, width=SHORT,
                         pauses=pauses)
                with pe.Fori(0, 2) as i:
                    for j in range(RING):
                        banks = 2 - 2 * (j // 2)

                        def free(m, j=j):
                            if j == 0:
                                pe.wait_ge(proj_ready, proj_no(l, 0) + i * 4)
                            if j == 2:
                                pe.wait_ge(proj_ready, proj_no(l, m + 1) + i * 4)
                        unit(l, 2 + j, rows_of(h_hi, j % 2), rows_of(h_lo, j % 2), banks, j % 2 == 0, j % 2 == 1,
                             it=i, free=free)
                for u in range(K_OUT - K_STRAIGHT):
                    k = K_STRAIGHT + u
                    pauses = {}
                    if 1 <= u <= NS:
                        pauses[0] = lambda: scores(l, u - 1)
                    if u < NS:
                        pauses[1] = lambda: t_job(l, "q", u)
                        if key_of(u):
                            pauses[3] = lambda: t_job(l, "k", u)
                    if 4 <= u <= NS + 1:
                        pauses[2] = lambda: transpose_probs(l, u - 2)
                        pauses[4] = lambda: values(l, u - 2)
                    if 5 <= u <= NS + 2:
                        pauses[5] = lambda: t_job(l, "o", u - 3)
                    if k < K_BRANCH:
                        e, r = k // 2, k % 2

                        def free(m):
                            if r == 0:
                                pe.wait_ge(proj_ready, proj_no(l, 2 * (e - 1) + m + 1))
                        unit(l, k, rows_of(h_hi, r), rows_of(h_lo, r), 0, r == 0, r == 1, free=free, pauses=pauses)
                        continue
                    r = k - K_BRANCH
                    b = BRANCH_INDEX[BRANCHES[r % 3]]
                    if r == 0:
                        pe.wait_ge(proj_ready, proj_no(l, 2 * CHUNKS))
                        pe.wait_ge(exp_done, (l + 1) * (4 * NS))
                    if r == 2:
                        pe.wait_ge(ot_lo, (l + 1) * NO)
                    elif r < 2:
                        pe.wait_ge(ot_lo, l * NO + 4 * (r + 1))

                    def free(m):
                        if r >= 2:
                            pe.wait_ge(part_ready, l * 12 + 2 * (r - 2) + m + 1)
                    if r == 4:
                        def merged_half():
                            pe.wait_ge(part_added, l * 8 + 4)
                            transpose_half(l, 1, 0, merged)
                        pauses[3] = merged_half
                    unit(l, k, rows_of(br_hi, b), rows_of(br_lo, b), 2 * (r % 2), True, True, free=free,
                         pauses=pauses)
                for r in range(4):
                    pauses = {}
                    if r == 0:
                        pe.wait_ge(half_lo, l * 12 + 6)
                    if r == 1:
                        def merged_half():
                            pe.wait_ge(part_added, l * 8 + 8)
                            transpose_half(l, 1, 1, merged)
                        pauses[2] = merged_half
                    if r == 2:
                        pe.wait_ge(half_lo, l * 12 + 8)
                    if r == 3:
                        def x_half():
                            pe.wait_ge(x_ready, l * 8 + 6)
                            transpose_half(l, 2, 0, xs)
                        pauses[3] = x_half

                    def free(m):
                        if r < 2:
                            pe.wait_ge(part_ready, l * 12 + 8 + 2 * r + m + 1)
                    unit(l, K_OUT + r, rows_of(h_hi, r // 2), rows_of(h_lo, r // 2), 2 * (r % 2), r < 2, r >= 2,
                         free=free, pauses=pauses)
                def up(k, it=None, chunk=None):
                    for r in range(2):
                        def free(m):
                            if r == 0 and chunk is not None:
                                pe.wait_ge(relu_ready, l * 2 * FFC + chunk * 2)
                        pauses = {}
                        if r == 0 and chunk is None:
                            def x_half():
                                pe.wait_ge(x_ready, l * 8 + 8)
                                transpose_half(l, 2, 1, xs)
                            pauses[1] = x_half
                        if chunk is None:
                            pe.wait_ge(half_lo, l * 12 + 10 + 2 * r)
                        unit(l, k + r, rows_of(h_hi, r), rows_of(h_lo, r), 0, r == 0, r == 1, it=it, free=free,
                             pauses=pauses)

                def transpose_hidden(chunk):
                    for m in range(MT):
                        pe.wait_ge(sq_ready, l * 2 * FFC + chunk * 2 + 2)
                    for b in range(2):
                        for a in range(2):
                            for m in range(MT):
                                kt = 2 * b + a
                                ins = pe.transpose(bank[6 + b][:, a * SEQ + m * P:a * SEQ + (m + 1) * P],
                                                   up_sq[:, m, kt * P:(kt + 1) * P], ident[:, :])
                        ins.then_inc(act_t, 1)

                def down(k, chunk, last, it=None):
                    pe.wait_ge(act_t_lo, l * 2 * FFC + chunk * 2 + 2)
                    for r in range(2):
                        unit(l, k + r, act_hi, act_lo, 2 + 2 * r, False, last, it=it)

                up(K_UP0)
                pe.wait_ge(zero_ready, 5)
                for n in range(2, 6):
                    pe.matmul(bank[n][:, :], ident_neg[:, :], zeros[:, :], start=True, stop=False)
                transpose_hidden(0)
                with pe.Fori(0, FFC - 1) as i:
                    up(K_LOOP, it=i, chunk=i + 1)
                    down(K_LOOP + 2, i, False, it=i)
                    transpose_hidden(i + 1)
                down(K_DOWN7, FFC - 1, True)


def rotation_table():
    import numpy as np
    inv = 1.0 / (np.float32(10000.0) ** (np.arange(0, HD, 2, dtype=np.float32) / np.float32(HD)))
    angle = np.arange(SEQ, dtype=np.float32)[:, None] * inv.astype(np.float32)[None, :]
    c, s = np.cos(angle), np.sin(angle)
    table = np.stack([np.concatenate([c, c], 1), np.concatenate([-s, s], 1)], 1)
    return np.ascontiguousarray(table.reshape(MT, P, 2, HD).transpose(1, 0, 2, 3).astype(np.float32))


def mask_table():
    import numpy as np
    row, key = np.arange(P)[:, None], np.arange(SEQ)[None, :]
    table = np.zeros((P, 2, 384), np.float32)
    for at, m, keys in ((0, 1, 256), (256, 0, 128)):
        diff = (row + m * P) - key[:, :keys]
        table[:, 0, at:at + keys] = diff < 0
        table[:, 1, at:at + keys] = (diff < 0) | (diff >= 128)
    return table


def kernel(x, norm1, w_in, sinks, w_branch, w_out, norm2, w_ff1, w_ff2, norm_f):
    import numpy as np
    import concourse.bacc as bacc
    from concourse.bass_utils import run_bass_kernel_spmd

    def features_on_rows(a):
        return a.reshape(LAYERS, KT, P).transpose(2, 0, 1).reshape(P, LAYERS * KT)

    nc = bacc.Bacc("TRN2", target_bir_lowering=False, num_devices=1)
    given = {"x": x, "norm1": features_on_rows(np.asarray(norm1)), "w_in": w_in, "sinks": sinks, "w_branch": w_branch, "w_out": w_out,
             "norm2": features_on_rows(np.asarray(norm2)), "w_ff1": w_ff1, "w_ff2": w_ff2, "norm_f": norm_f,
             "rope": rotation_table(), "masks": mask_table(), "identity": np.eye(P, dtype=np.float32)}
    arrays = {f"in_{n}": np.ascontiguousarray(a) for n, a in given.items()}
    aps = [nc.dram_tensor(n, a.shape, F32, kind="ExternalInput").ap() for n, a in arrays.items()]
    out = nc.dram_tensor("out_0", (1, SEQ, D), F32, kind="ExternalOutput").ap()
    program(nc, *aps, out)
    result = run_bass_kernel_spmd(nc, [arrays], core_ids=[0])
    return result.results[0]["out_0"]
```

```python
from contextlib import ExitStack

import concourse.bass as bass
from concourse import mybir

F32 = mybir.dt.float32
F32R = mybir.dt.float32r
BF16 = mybir.dt.bfloat16
ALU = mybir.AluOpType
ACT = mybir.ActivationFunctionType
AX = mybir.AxisListType

P = 128
SEQ = 256
MT = SEQ // P
D = 1024
KT = D // P
HD = 64
DFF = 4096
LAYERS = 2
EPS = 1e-6
QKV = 3268
GATES = 3 * D
N_IN = QKV + GATES
CW = 512
KU = 4
SHORT = QKV % CW
QKV_CHUNKS = 1 + QKV // CW
CHUNKS = QKV_CHUNKS + GATES // CW
RING = 4
RAW = 2
FFC = DFF // CW

K_STRAIGHT = 10
K_GATES = 2 * QKV_CHUNKS
K_BRANCH = K_GATES + 2 * (GATES // CW)
K_OUT = K_BRANCH + 6
K_UP0 = K_OUT + 4
K_UP1 = K_UP0 + 2
K_LOOP = K_UP1 + RING
MLP_ROUNDS = (FFC - 2) // 2
K_DOWN7 = K_UP1 + RING * (FFC - 1)
UNITS = K_DOWN7 + 2
assert UNITS % RING == 0 and FFC % 2 == 0 and K_DOWN7 == K_LOOP + 2 * RING * MLP_ROUNDS

A_Q, A_K, A_V = 0, 512, 576
I_Q, I_K, I_W = 640, 896, 960
B_Q, B_K, B_V = 964, 1476, 1604
C_Q, C_K, C_V = 1732, 2244, 2756

SCALE = HD ** -0.5
IDX_SCALE = (64 ** -0.5) * (4 ** -0.5)
TOPK = SEQ // 4
ROUNDS = TOPK // 8
TAKEN = -3.0e38
MASKED = -1.0e30

STEPS = [("i", 0), ("i", 1)] + [(b, p) for b in "bca" for p in range(4)]
NS = len(STEPS)
Q_COL = {"a": A_Q, "i": I_Q, "b": B_Q, "c": C_Q}
BRANCHES = "bca"
BRANCH_INDEX = {"a": 0, "b": 1, "c": 2}
FIRST_A = STEPS.index(("a", 0))


def key_of(step):
    b, p = STEPS[step]
    if b == "i":
        return (I_K, 1) if p == 0 else None
    if b == "a":
        return (A_K, 1) if p == 0 else None
    if b == "b":
        return (B_K + HD * (p // 2), 1) if p % 2 == 0 else None
    return C_K + P * p, 2


KEY_JOB = {}
for _s in range(NS):
    KEY_JOB[_s] = (KEY_JOB[_s - 1] if _s else -1) + (key_of(_s) is not None)

T_JOBS = []
for _u in range(NS + 3):
    if _u < NS:
        T_JOBS.append(("q", _u))
        if key_of(_u):
            T_JOBS.append(("k", _u))
    if _u - 3 >= 2:
        T_JOBS.append(("o", _u - 3))
NT = len(T_JOBS)
NO = NS - 2


def width_of(k, it):
    return SHORT if it is None and k < 2 else CW


def value_col(branch, head):
    return {"a": A_V, "b": B_V + HD * (head // 4), "c": C_V + HD * head}[branch]


def program(nc, x, norm1, w_in, sinks, w_branch, w_out, norm2, w_ff1, w_ff2, norm_f, rope, masks,
            identity, out):
    win_v = w_in.rearrange("l (k p) n -> p (l k) n", p=P)
    wbr_v = w_branch.rearrange("l b (k p) n -> p (l b k) n", p=P)
    wout_v = w_out.rearrange("l (k p) n -> p (l k) n", p=P)
    wup_v = w_ff1.rearrange("l (k p) n -> p (l k) n", p=P)
    wdown_v = w_ff2.rearrange("l (k p) n -> p (l k) n", p=P)
    x_v = x.rearrange("b (m p) d -> p (b m) d", p=P)
    out_v = out.rearrange("b (m p) d -> p (b m) d", p=P)

    with ExitStack() as ctx:
        def sb(name, shape, dt=F32):
            return ctx.enter_context(nc.sbuf_tensor(name, shape, dt))

        def sem(name):
            return ctx.enter_context(nc.semaphore(name))

        bank = [ctx.enter_context(nc.psum_tensor(f"bank{i}", [P, 512], F32)) for i in range(8)]

        raw = sb("raw", [P, RAW, KU, CW])
        w_hi = sb("w_hi", [P, RING, KU, CW], F32R)
        w_lo = sb("w_lo", [P, RING, KU, CW], F32R)
        xs = sb("xs", [P, MT, D])
        h_hi = sb("h_hi", [P, KT, SEQ], F32R)
        h_lo = sb("h_lo", [P, KT, SEQ], F32R)
        br_hi = sb("br_hi", [P, 12, SEQ], F32R)
        br_lo = sb("br_lo", [P, 12, SEQ], F32R)
        act_hi = [br_hi[:, KU * n:KU * (n + 1), :] for n in range(2)]
        act_lo = [br_lo[:, KU * n:KU * (n + 1), :] for n in range(2)]
        proj = sb("proj", [P, MT, QKV])
        merged = proj[:, :, 0:D]
        gate = sb("gate", [P, MT, GATES])
        gate_flat = gate[:, :, :].rearrange("p m n -> p (m n)")
        rt1 = gate_flat[:, 0:1280]
        rt2 = gate_flat[:, 1280:2560]
        relu_dots = gate_flat[:, 2560:2560 + 4 * 384].rearrange("p (h n) -> p h n", h=4)
        score = gate_flat[:, 5632:6016]
        picked = gate_flat[:, 5120:5504]
        up_relu = gate_flat[:, 0:1024].rearrange("p (m n) -> p m n", m=MT)
        up_sq = gate_flat[:, 1024:2048].rearrange("p (m n) -> p m n", m=MT)
        squares = gate_flat[:, 2048:4096].rearrange("p (m n) -> p m n", m=MT)
        gain_f = gate_flat[:, 4096:5120]
        mask_f = gate_flat[:, 4096:4864].rearrange("p (a n) -> p a n", a=2)
        normed = gate_flat[:, 0:2048].rearrange("p (m n) -> p m n", m=MT)
        q_t = sb("q_t", [P, 2, SEQ])
        k_t = sb("k_t", [P, 2, SEQ])
        k_pair = sb("k_pair", [P, 4, MT, P])
        prob = sb("prob", [P, 2, 768])
        part = prob[:, :, :].rearrange("p a n -> p (a n)")[:, 0:1024].rearrange("p (m n) -> p m n", m=MT)
        prob_t = sb("prob_t", [P, 768])
        o_sb = sb("o_sb", [P, 2, 2, P])
        rope_sb = sb("rope_sb", [P, MT, 2, HD])
        causal_f = sb("causal_f", [P, 384])
        mask_b = sb("mask_b", [P, 3, 384], BF16)
        table_out = sb("table_out", [P, 1])
        causal_bias = sb("causal_bias", [P, 384])
        ident = sb("ident", [P, P])
        ident_neg = sb("ident_neg", [P, P], BF16)
        zeros = sb("zeros", [P, CW], BF16)
        top8 = sb("top8", [P, 2, 8])
        gain = sb("gain", [P, 2, KT])
        sink_neg = sb("sink_neg", [P, 8])
        sink_raw = sb("sink_raw", [P, 8])
        consts = sb("consts", [P, 3, MT])
        ssq = sb("ssq", [P, 2, MT])
        var = sb("var", [P, 2, MT])
        rstd = sb("rstd", [P, MT])
        rstd_half = sb("rstd_half", [P, MT])
        row_max = sb("row_max", [P, 2, 4])
        neg_max = sb("neg_max", [P, 2, 4])
        row_sum = sb("row_sum", [P, 2, 4])
        sink_arg = sb("sink_arg", [P, 2, 4])
        sink_exp = sb("sink_exp", [P, 2, 4])
        row_inv = sb("row_inv", [P, 2, 4])

        raw_in = [sem(f"raw_in{i}") for i in range(RAW)]
        x_in = [sem(f"x_in{c}") for c in range(2)]
        ident_in, const_in, small_in, out_sent, gf_in = (sem(n) for n in (
            "ident_in", "const_in", "small_in", "out_sent", "gf_in"))
        hi_ready = sem("hi_ready")
        lo_ready = sem("lo_ready")
        mm_done = sem("mm_done")
        x_ready = sem("x_ready")
        const_ready = sem("const_ready")
        consts_set = sem("consts_set")
        zero_ready = sem("zero_ready")
        half_t = sem("half_t")
        half_hi = sem("half_hi")
        half_lo = sem("half_lo")
        ssq_ready = sem("ssq_ready")
        rstd_ready = sem("rstd_ready")
        proj_ready = sem("proj_ready")
        rope_done = sem("rope_done")
        t_done = sem("t_done")
        t_taken = sem("t_taken")
        ot_lo = sem("ot_lo")
        s_done = sem("s_done")
        neg_ready = sem("neg_ready")
        exp_done = sem("exp_done")
        sink_arg_ready = sem("sink_arg_ready")
        sink_exp_ready = sem("sink_exp_ready")
        pt_done = sem("pt_done")
        pt1_taken = sem("pt1_taken")
        pt0_taken = sem("pt0_taken")
        pv_done = sem("pv_done")
        o_ready = sem("o_ready")
        chosen = sem("chosen")
        part_ready = sem("part_ready")
        part_added = sem("part_added")
        relu_ready = sem("relu_ready")
        sq_ready = sem("sq_ready")
        act_t = sem("act_t")
        act_t_hi = sem("act_t_hi")
        act_t_lo = sem("act_t_lo")
        dve_step = sem("dve_step")
        pool_step = sem("pool_step")
        gained = [sem(f"gained{c}") for c in range(2)]
        y_ready = [sem(f"y_ready{m}") for m in range(MT)]
        table_ready = sem("table_ready")
        wait_passed = sem("wait_passed")

        def proj_no(l, n):
            return l * (2 * CHUNKS) + (n + 1)

        def unit_no(l, k, it=None):
            n = l * UNITS + k
            return n if it is None else n + it * RING

        def half_no(l, k, m, it=None):
            n = l * (2 * UNITS) + (2 * k + m + 1 + 2 * RING)
            return n if it is None else n + it * (2 * RING)

        class Count:
            def __init__(self, per_layer):
                self.per_layer, self.n = per_layer, 0

            def one_more(self):
                self.n += 1
                return 1

            def value(self, l, n=None):
                return l * self.per_layer + (self.n if n is None else n)

        CONSTS = 4
        DVE_PER_LAYER = 1 + 2 * 4 + 1 + 4 * ROUNDS + 4 * NO + 4 + NO
        POOL_PER_LAYER = 2 * 3 + 5

        block = ctx.enter_context(nc.Block())

        @block.sync
        def _(sp):
            sp.sem_inc(lo_ready, RAW)
            sp.dma_start(xs[:, :, 0:CW], x_v[:, :, 0:CW]).then_inc(x_in[0], 16)

            def load(l, k, source, it=None, width=CW):
                sp.wait_ge(lo_ready, unit_no(l, k, it) + 1)
                sp.dma_start(raw[:, k % RAW, :, 0:width], source).then_inc(raw_in[k % RAW], 16)

            with sp.Fori(0, LAYERS) as l:
                sp.wait_ge(lo_ready, unit_no(l, 0) + 1)
                sp.dma_start(gain[:, 0, :], norm1[:, bass.ds(l * KT, KT)]).then_inc(small_in, 16)
                sp.dma_start(gain[:, 1, :], norm2[:, bass.ds(l * KT, KT)]).then_inc(small_in, 16)
                sp.dma_start(sink_raw[:, :], sinks[bass.ds(l, 1), :].to_broadcast([P, 8])).then_inc(small_in, 16)

                for r in range(2):
                    load(l, r, win_v[:, bass.ds(l * KT + r * KU, KU), 0:SHORT], width=SHORT)
                with sp.Fori(0, (K_BRANCH - 2) // RING) as i:
                    for j in range(RING):
                        col = i * (2 * CW) + (SHORT + (j // 2) * CW)
                        load(l, 2 + j, win_v[:, bass.ds(l * KT + (j % 2) * KU, KU), bass.ds(col, CW)], it=i)
                for r in range(6):
                    c, b = r // 3, BRANCH_INDEX[BRANCHES[r % 3]]
                    load(l, K_BRANCH + r, wbr_v[:, bass.ds(l * 12 + b * KU, KU), c * CW:(c + 1) * CW])
                for r in range(4):
                    load(l, K_OUT + r, wout_v[:, bass.ds(l * KT + (r // 2) * KU, KU),
                                              (r % 2) * CW:(r % 2 + 1) * CW])
                for r in range(2):
                    load(l, K_UP0 + r, wup_v[:, bass.ds(l * KT + r * KU, KU), 0:CW])
                with sp.Fori(0, FFC - 1) as i:
                    for r in range(2):
                        load(l, K_UP1 + r, wup_v[:, bass.ds(l * KT + r * KU, KU), bass.ds((i + 1) * CW, CW)],
                             it=i)
                    for r in range(2):
                        load(l, K_UP1 + 2 + r, wdown_v[:, bass.ds(l * (DFF // P) + i * KU, KU),
                                                        r * CW:(r + 1) * CW], it=i)
                for r in range(2):
                    load(l, K_DOWN7 + r, wdown_v[:, bass.ds(l * (DFF // P) + (FFC - 1) * KU, KU),
                                                 r * CW:(r + 1) * CW])
            sp.wait_ge(act_t, 2 * FFC * LAYERS)
            sp.dma_start(gain_f, norm_f.rearrange("(o n) -> o n", o=1).to_broadcast([P, D])).then_inc(gf_in, 16)
            for c in range(2):
                sp.wait_ge(y_ready[0], c + 1)
                sp.dma_start(out_v[:, 0, c * CW:(c + 1) * CW],
                             normed[:, 0, c * CW:(c + 1) * CW]).then_inc(out_sent, 16)
            sp.wait_ge(out_sent, 16 * 2 * MT)

        @block.scalar
        def _(act):
            act.sem_inc(proj_ready, 1)
            act.dma_start(ident[:, :], identity).then_inc(ident_in, 16)
            act.wait_ge(zero_ready, 1)
            act.activation(table_out[:, :], zeros[:, 0:1], ACT.Exp).then_inc(table_ready, 1)
            act.wait_ge(x_in[0], 16)
            act.dma_start(xs[:, :, CW:D], x_v[:, :, CW:D]).then_inc(x_in[1], 16)
            act.dma_start(rope_sb[:, :, :, :], rope).then_inc(const_in, 16)
            act.dma_start(mask_f, masks).then_inc(const_in, 16)

            def high(l, k, it=None):
                width = width_of(k, it)
                n = l * (UNITS // RAW) + (k // RAW + 1)
                if it is not None:
                    n = n + it * (RING // RAW)
                act.wait_ge(raw_in[k % RAW], n * 16)
                act.wait_ge(mm_done, half_no(l, k - RING, 1, it))
                act.activation(w_hi[:, k % RING, :, 0:width], raw[:, k % RAW, :, 0:width],
                               ACT.Copy).then_inc(hi_ready, 1)

            def half_high(l, group, c, gains):
                for b in range(2):
                    act.wait_ge(half_t, l * 12 + (4 * group + 2 * c + b + 1))
                    src = bank[(6, 4)[c] + b]
                    kt = 4 * c + 2 * b
                    if gains is None:
                        act.activation(h_hi[:, kt:kt + 2, :], src[:, :].rearrange("p (a n) -> p a n", a=2),
                                       ACT.Copy, scale=0.5).then_inc(half_hi, 1)
                    else:
                        act.activation(h_hi[:, kt, :], src[:, 0:SEQ], ACT.Identity, bias=0.0,
                                       scale=gain[:, gains, kt:kt + 1])
                        act.activation(h_hi[:, kt + 1, :], src[:, SEQ:512], ACT.Identity, bias=0.0,
                                       scale=gain[:, gains, kt + 1:kt + 2]).then_inc(half_hi, 1)

            def sum_squares(l, which):
                for c in range(2):
                    act.wait_ge(x_ready, l * 8 + 4 * which + 2 * c + 2)
                    for m in range(MT):
                        act.activation(squares[:, m, c * CW:(c + 1) * CW], xs[:, m, c * CW:(c + 1) * CW],
                                       ACT.Square, scale=D ** -0.5, accum_out=ssq[:, c, m:m + 1]).then_inc(ssq_ready, 1)

            def take_proj(l, e, k, m, it=None):
                act.wait_ge(mm_done, half_no(l, k, m, it))
                src = bank[(2 * (e % 2) if e < 5 else 0) + m]
                if e < QKV_CHUNKS:
                    width = width_of(k, it)
                    col = e * CW - (CW - SHORT if e else 0)
                    act.activation(proj[:, m, col:col + width], src[:, 0:width], ACT.Identity, bias=0.0,
                                   scale=rstd[:, m:m + 1]).then_inc(proj_ready, 1)
                else:
                    g = e - QKV_CHUNKS
                    act.activation(gate[:, m, g * CW:(g + 1) * CW], src[:, :], ACT.Tanh, bias=0.0,
                                   scale=rstd_half[:, m:m + 1]).then_inc(proj_ready, 1)

            def take_t(l, kind, step):
                j = T_JOBS.index((kind, step))
                act.wait_ge(t_done, l * NT + j + 1)
                src = bank[6][:, 0:SEQ]
                if kind == "q":
                    act.activation(q_t[:, step % 2, :], src, ACT.Copy).then_inc(t_taken, 1)
                elif kind == "k":
                    act.activation(k_t[:, KEY_JOB[step] % 2, :], src, ACT.Copy).then_inc(t_taken, 1)
                else:
                    b, p = STEPS[step]
                    act.activation(br_hi[:, 4 * BRANCH_INDEX[b] + p, :], src, ACT.Copy).then_inc(t_taken, 1)

            def exponentials(l, s):
                par = s % 2
                act.wait_ge(s_done, l * 2 * NS + 2 * s + 2)
                if s < 2:
                    for j in range(2):
                        act.activation(relu_dots[:, 2 * s + j, :], bank[2 + j][:, 0:384],
                                       ACT.Relu).then_inc(exp_done, 2)
                    return
                act.wait_ge(neg_ready, l * NO + (s - 2) + 1)
                for n in range(4):
                    lo, w = (0, 256) if n < 2 else (256, 128)
                    act.activation(prob[:, par, 384 * (n % 2) + lo:384 * (n % 2) + lo + w],
                                   bank[2 + n % 2][:, lo:lo + w], ACT.Exp, bias=neg_max[:, par, n:n + 1],
                                   scale=SCALE, accum_out=row_sum[:, par, n:n + 1]).then_inc(exp_done, 1)
                if STEPS[s][0] == "b":
                    act.wait_ge(sink_arg_ready, l * 4 + (s - 2) + 1)
                    act.activation(sink_exp[:, par, :], sink_arg[:, par, :], ACT.Exp).then_inc(sink_exp_ready, 1)

            def take_probs(l, s):
                act.wait_ge(pt_done, l * 2 * NO + 2 * (s - 2) + 1)
                act.activation(prob_t[:, 0:512], bank[4][:, :], ACT.Copy).then_inc(pt1_taken, 1)

            def hidden_high(l, chunk, parity):
                for b in range(2):
                    act.wait_ge(act_t, l * 2 * FFC + chunk * 2 + b + 1)
                    act.activation(act_hi[parity][:, 2 * b:2 * b + 2, :],
                                   bank[6 + b][:, :].rearrange("p (a n) -> p a n", a=2),
                                   ACT.Copy).then_inc(act_t_hi, 1)

            def take_up(l, k, chunk, it=None, first_chunk=False):
                for m in range(MT):
                    act.wait_ge(mm_done, half_no(l, k + 1, m, it))
                    if not first_chunk:
                        act.wait_ge(sq_ready, l * 2 * FFC + chunk * 2)
                    act.activation(up_relu[:, m, :], bank[m][:, :], ACT.Relu,
                                   scale=rstd[:, m:m + 1]).then_inc(relu_ready, 1)

            with act.Fori(0, LAYERS) as l:
                high(l, 0)
                act.wait_ge(small_in, l * 48 + 48)
                half_high(l, 0, 0, 0)
                high(l, 1)
                half_high(l, 0, 1, 0)
                high(l, 2)
                sum_squares(l, 0)
                high(l, 3)
                act.wait_ge(rstd_ready, l * 2 + 1)
                for m in range(MT):
                    take_proj(l, 0, 1, m)
                with act.Fori(0, 2) as i:
                    for j in range(2):
                        high(l, 4 + 2 * j, it=i)
                        high(l, 5 + 2 * j, it=i)
                        for m in range(MT):
                            act.wait_ge(mm_done, half_no(l, 3 + 2 * j, m, i))
                            act.activation(proj[:, m, bass.ds(i * (2 * CW) + (SHORT + j * CW), CW)],
                                           bank[2 * (1 - j) + m][:, :], ACT.Identity, bias=0.0,
                                           scale=rstd[:, m:m + 1]).then_inc(proj_ready, 1)
                for u in range(K_OUT - K_STRAIGHT):
                    k = K_STRAIGHT + u
                    high(l, k + 2)
                    if u < NS:
                        take_t(l, "q", u)
                    if 1 <= u <= NS:
                        exponentials(l, u - 1)
                    if 4 <= u <= NS + 1:
                        take_probs(l, u - 2)
                    last = k < K_BRANCH and k % 2 == 1
                    e = k // 2
                    if k == K_GATES + 1:
                        act.wait_ge(rope_done, l * 5 + 5)
                        act.wait_ge(chosen, l * 2 + 1)
                    if k == K_GATES + 9:
                        act.wait_ge(chosen, l * 2 + 2)
                    if last:
                        take_proj(l, e, k, 0)
                    if u < NS and key_of(u):
                        take_t(l, "k", u)
                    if last:
                        take_proj(l, e, k, 1)
                    if 5 <= u <= NS + 2:
                        take_t(l, "o", u - 3)
                    if k == K_BRANCH + 4:
                        half_high(l, 1, 0, None)
                high(l, K_OUT + 2)
                high(l, K_OUT + 3)
                half_high(l, 1, 1, None)
                high(l, K_OUT + 4)
                high(l, K_OUT + 5)
                half_high(l, 2, 0, 1)
                half_high(l, 2, 1, 1)
                sum_squares(l, 1)
                high(l, K_UP1)
                high(l, K_UP1 + 1)
                act.wait_ge(rstd_ready, l * 2 + 2)
                take_up(l, K_UP0, 0, first_chunk=True)
                high(l, K_UP1 + 2)
                hidden_high(l, 0, 0)
                high(l, K_UP1 + 3)
                take_up(l, K_UP1, 1)
                high(l, K_UP1 + 4)
                hidden_high(l, 1, 1)
                high(l, K_UP1 + 5)
                with act.Fori(0, MLP_ROUNDS) as i:
                    for a in range(2):
                        k = K_LOOP + RING * a
                        high(l, k + 2, it=i * 2)
                        high(l, k + 3, it=i * 2)
                        take_up(l, k, i * 2 + (2 + a), it=i * 2)
                        high(l, k + 4, it=i * 2)
                        hidden_high(l, i * 2 + (2 + a), a)
                        high(l, k + 5, it=i * 2)
            sum_squares(LAYERS - 1, 2)
            act.wait_ge(rstd_ready, 2 * LAYERS + 1)
            for c in range(2):
                act.wait_ge(gained[c], MT)
                cols = normed[:, 1, c * CW:(c + 1) * CW]
                act.activation(cols, cols, ACT.Identity, bias=0.0, scale=rstd[:, 1:2]).then_inc(y_ready[1], 1)
                act.wait_ge(y_ready[1], c + 1)
                act.dma_start(out_v[:, 1, c * CW:(c + 1) * CW], cols).then_inc(out_sent, 16)

        @block.vector
        def _(dve):
            dve.memset(zeros[:, :], 0.0).then_inc(zero_ready, 1)
            dve.wait_ge(x_in[0], 16)
            dve.sem_inc(x_ready, 2)

            def low(l, k, it=None):
                width = width_of(k, it)
                dve.wait_ge(hi_ready, unit_no(l, k, it) + 1)
                dve.tensor_tensor(w_lo[:, k % RING, :, 0:width], raw[:, k % RAW, :, 0:width],
                                  w_hi[:, k % RING, :, 0:width].bitcast(F32),
                                  ALU.subtract).then_inc(lo_ready, 1)

            def half_low(l, group, c, gains):
                for b in range(2):
                    dve.wait_ge(half_hi, l * 12 + (4 * group + 2 * c + b + 1))
                    src = bank[(6, 4)[c] + b]
                    kt = 4 * c + 2 * b
                    if gains is None:
                        dve.scalar_tensor_tensor(
                            h_lo[:, kt:kt + 2, :], src[:, :].rearrange("p (a n) -> p a n", a=2), 0.5,
                            h_hi[:, kt:kt + 2, :].bitcast(F32), ALU.mult, ALU.subtract).then_inc(half_lo, 1)
                        continue
                    for a in range(2):
                        ins = dve.scalar_tensor_tensor(
                            h_lo[:, kt + a, :], src[:, a * SEQ:(a + 1) * SEQ], gain[:, gains, kt + a:kt + a + 1],
                            h_hi[:, kt + a, :].bitcast(F32), ALU.mult, ALU.subtract)
                    ins.then_inc(half_lo, 1)

            def add_to_x(l, c, k, banks):
                for m in range(MT):
                    dve.wait_ge(mm_done, half_no(l, k, m))
                    cols = xs[:, m, c * CW:(c + 1) * CW]
                    dve.tensor_tensor(cols, cols, bank[banks + m][:, :], ALU.add).then_inc(x_ready, 1)

            def maxima(l, own, s):
                par, b = s % 2, STEPS[s][0]
                dve.wait_ge(s_done, l * 2 * NS + 2 * s + 2)
                for n in range(4):
                    lo, w = (0, 256) if n < 2 else (256, 128)
                    dve.tensor_reduce(row_max[:, par, n:n + 1], bank[2 + n % 2][:, lo:lo + w],
                                      AX.X, ALU.max).then_inc(dve_step, own.one_more())
                dve.wait_ge(dve_step, own.value(l))
                if b != "b":
                    dve.tensor_scalar(neg_max[:, par, :], row_max[:, par, :], -SCALE, None,
                                      ALU.mult).then_inc(neg_ready, 1)
                    return
                p = STEPS[s][1]
                sk = sink_neg[:, 2 * p:2 * p + 2].unsqueeze(1).to_broadcast([P, 2, 2])
                dve.scalar_tensor_tensor(
                    neg_max[:, par, :].rearrange("p (m h) -> p m h", m=2),
                    row_max[:, par, :].rearrange("p (m h) -> p m h", m=2), -SCALE, sk,
                    ALU.mult, ALU.min).then_inc(neg_ready, 1)
                dve.wait_ge(neg_ready, l * NO + (s - 2) + 1)
                dve.tensor_tensor(sink_arg[:, par, :].rearrange("p (m h) -> p m h", m=2),
                                  neg_max[:, par, :].rearrange("p (m h) -> p m h", m=2), sk,
                                  ALU.subtract).then_inc(sink_arg_ready, 1)

            def take_probs(l, s):
                dve.wait_ge(pt_done, l * 2 * NO + 2 * (s - 2) + 2)
                dve.tensor_copy(prob_t[:, 512:768], bank[5][:, 0:256]).then_inc(pt0_taken, 1)

            def inverse_sums(l, own, s):
                par = s % 2
                dve.wait_ge(exp_done, l * 4 * NS + 4 * s + 4)
                if STEPS[s][0] == "b":
                    dve.wait_ge(sink_exp_ready, l * 4 + (s - 2) + 1)
                    dve.tensor_tensor(row_sum[:, par, :], row_sum[:, par, :], sink_exp[:, par, :],
                                      ALU.add).then_inc(dve_step, own.one_more())
                    dve.wait_ge(dve_step, own.value(l))
                dve.reciprocal(row_inv[:, par, :], row_sum[:, par, :]).then_inc(dve_step, own.one_more())
                return own.n

            def normalise(l, own, s, n):
                par = s % 2
                dve.wait_ge(pv_done, l * NO + (s - 2) + 1)
                dve.wait_ge(dve_step, own.value(l, n))
                dve.tensor_tensor(
                    o_sb[:, par, :, :].rearrange("p m (h d) -> p (m h) d", h=2),
                    bank[7][:, 0:256].rearrange("p (a d) -> p a d", a=4),
                    row_inv[:, par, :].unsqueeze(2).to_broadcast([P, 4, HD]), ALU.mult).then_inc(o_ready, 1)

            def out_low(l, s):
                b, p = STEPS[s]
                j = T_JOBS.index(("o", s))
                dve.wait_ge(t_taken, l * NT + j + 1)
                kt = 4 * BRANCH_INDEX[b] + p
                dve.tensor_tensor(br_lo[:, kt, :], bank[6][:, 0:SEQ], br_hi[:, kt, :].bitcast(F32),
                                  ALU.subtract).then_inc(ot_lo, 1)

            def index_scores(l, own, s):
                dve.wait_ge(exp_done, l * 4 * NS + 4 * s + 4)
                for j in range(2):
                    h = 2 * s + j
                    for m, lo, w in ((1, 0, 256), (0, 256, 128)):
                        cols = score[:, lo:lo + w]
                        wt = proj[:, m, I_W + h:I_W + h + 1]
                        if h == 0:
                            dve.tensor_scalar(cols, relu_dots[:, h, lo:lo + w], wt, None,
                                              ALU.mult).then_inc(dve_step, own.one_more())
                        else:
                            dve.wait_ge(dve_step, own.value(l, own.n - 1))
                            dve.scalar_tensor_tensor(cols, relu_dots[:, h, lo:lo + w], wt, cols, ALU.mult,
                                                     ALU.add).then_inc(dve_step, own.one_more())

            def settled(l, own):
                dve.wait_ge(dve_step, own.value(l))
                dve.sem_inc(wait_passed, 1)

            def top_round(l, own):
                spans = ((0, 0, 256), (1, 256, 128))
                settled(l, own)
                for m, lo, w in spans:
                    dve.max(top8[:, m, :], picked[:, lo:lo + w]).then_inc(dve_step, own.one_more())
                settled(l, own)
                for m, lo, w in spans:
                    dve.match_replace(picked[:, lo:lo + w], top8[:, m, :], picked[:, lo:lo + w],
                                      TAKEN).then_inc(dve_step, own.one_more())

            with dve.Fori(0, LAYERS) as l:
                own = Count(DVE_PER_LAYER)
                low(l, 0)
                dve.wait_ge(small_in, l * 48 + 48)
                half_low(l, 0, 0, 0)
                low(l, 1)
                half_low(l, 0, 1, 0)
                low(l, 2)
                dve.tensor_scalar(sink_neg[:, :], sink_raw[:, :], -1.0, None,
                                  ALU.mult).then_inc(dve_step, own.one_more())
                low(l, 3)
                with dve.Fori(0, 2) as i:
                    for j in range(RING):
                        low(l, 4 + j, it=i)
                inverse = {}
                for u in range(K_OUT - K_STRAIGHT):
                    k = K_STRAIGHT + u
                    if 3 <= u <= NS:
                        maxima(l, own, u - 1)
                    low(l, k + 2)
                    if 1 <= u <= 2:
                        index_scores(l, own, u - 1)
                    if u == 2:
                        dve.wait_ge(const_ready, CONSTS)
                        dve.wait_ge(dve_step, own.value(l))
                        dve.scalar_tensor_tensor(picked[:, :], score[:, :], IDX_SCALE, causal_bias[:, :],
                                                 ALU.mult, ALU.add).then_inc(dve_step, own.one_more())
                        dve.wait_ge(dve_step, own.value(l))
                        dve.sem_inc(chosen, 1)
                    if 4 <= u <= NS + 1:
                        take_probs(l, u - 2)
                        inverse[u - 2] = inverse_sums(l, own, u - 2)
                    if 3 <= u < 3 + ROUNDS:
                        top_round(l, own)
                    if u == FIRST_A:
                        dve.wait_ge(dve_step, own.value(l))
                        dve.scalar_tensor_tensor(mask_b[:, 2, :], picked[:, :], TAKEN, causal_f[:, :],
                                                 ALU.is_gt, ALU.add).then_inc(chosen, 1)
                    if 4 <= u <= NS + 1:
                        normalise(l, own, u - 2, inverse[u - 2])
                    if 5 <= u <= NS + 2:
                        out_low(l, u - 3)
                    if k >= K_BRANCH:
                        r = k - K_BRANCH
                        c, b = r // 3, BRANCH_INDEX[BRANCHES[r % 3]]
                        for m in range(MT):
                            dve.wait_ge(mm_done, half_no(l, k, m))
                            dve.wait_ge(proj_ready, proj_no(l, 2 * CHUNKS))
                            dst = merged[:, m, c * CW:(c + 1) * CW] if r % 3 == 0 else part[:, m, :]
                            if r % 3:
                                prior = 2 * (2 * c + r % 3 - 1) - 2 + m + 1
                                if prior > 0:
                                    dve.wait_ge(part_added, l * 8 + prior)
                            dve.scalar_tensor_tensor(dst, gate[:, m, b * D + c * CW:b * D + (c + 1) * CW], 1.0,
                                                     bank[2 * (r % 2) + m][:, :], ALU.add,
                                                     ALU.mult).then_inc(part_ready, 1)
                    if k == K_BRANCH + 4:
                        half_low(l, 1, 0, None)
                assert own.n == DVE_PER_LAYER, (own.n, DVE_PER_LAYER)
                low(l, K_OUT + 2)
                low(l, K_OUT + 3)
                half_low(l, 1, 1, None)
                low(l, K_OUT + 4)
                add_to_x(l, 0, K_OUT + 2, 0)
                low(l, K_OUT + 5)
                half_low(l, 2, 0, 1)
                add_to_x(l, 1, K_OUT + 3, 2)
                half_low(l, 2, 1, 1)

                def hidden_low(chunk, parity):
                    for b in range(2):
                        dve.wait_ge(act_t_hi, l * 2 * FFC + chunk * 2 + b + 1)
                        dve.tensor_tensor(act_lo[parity][:, 2 * b:2 * b + 2, :],
                                          bank[6 + b][:, :].rearrange("p (a n) -> p a n", a=2),
                                          act_hi[parity][:, 2 * b:2 * b + 2, :].bitcast(F32),
                                          ALU.subtract).then_inc(act_t_lo, 1)

                for j in range(3):
                    low(l, K_UP1 + j)
                hidden_low(0, 0)
                low(l, K_UP1 + 3)
                low(l, K_UP1 + 4)
                hidden_low(1, 1)
                low(l, K_UP1 + 5)
                with dve.Fori(0, MLP_ROUNDS) as i:
                    for a in range(2):
                        for j in range(3):
                            low(l, K_LOOP + RING * a + 2 + j, it=i * 2)
                        hidden_low(i * 2 + (2 + a), a)
                        low(l, K_LOOP + RING * a + 5, it=i * 2)
                add_to_x(l, 0, K_DOWN7, 2)
                add_to_x(l, 1, K_DOWN7 + 1, 4)
            dve.wait_ge(gf_in, 16)
            dve.wait_ge(x_ready, LAYERS * 8 + 4)
            for m in range(MT):
                dve.tensor_tensor(normed[:, m, CW:D], xs[:, m, CW:D], gain_f[:, CW:D],
                                  ALU.mult).then_inc(gained[1], 1)
            dve.wait_ge(rstd_ready, 2 * LAYERS + 1)
            for c in range(2):
                dve.wait_ge(gained[c], 1)
                cols = normed[:, 0, c * CW:(c + 1) * CW]
                dve.tensor_scalar(cols, cols, rstd[:, 0:1], None, ALU.mult).then_inc(y_ready[0], 1)

        @block.gpsimd
        def _(pool):
            for n, value in enumerate((-0.5, 0.5, EPS)):
                pool.memset(consts[:, n, :], value).then_inc(consts_set, 1)
            pool.wait_ge(consts_set, 3)
            pool.wait_ge(ident_in, 16)
            pool.tensor_scalar(ident_neg[:, :], ident[:, :], MASKED, None, ALU.mult).then_inc(const_ready, 1)
            pool.wait_ge(x_in[1], 16)
            pool.wait_ge(x_ready, 2)
            pool.sem_inc(x_ready, 2)
            pool.wait_ge(const_in, 32)
            pool.tensor_copy(mask_b[:, 0:2, :], mask_f).then_inc(const_ready, 1)
            pool.tensor_copy(causal_f[:, :], mask_f[:, 0, :]).then_inc(const_ready, 1)
            pool.tensor_scalar(causal_bias[:, :], mask_f[:, 0, :], MASKED, None, ALU.mult).then_inc(const_ready, 1)

            def inverse_rms(count, done, final=False):
                pool.wait_ge(ssq_ready, count * 4)
                pool.tensor_tensor(var[:, 0, :], ssq[:, 0, :], ssq[:, 1, :], ALU.add).then_inc(pool_step, 1)
                pool.wait_ge(pool_step, done(1))
                pool.tensor_tensor(var[:, 1, :], var[:, 0, :], consts[:, 2, :], ALU.add).then_inc(pool_step, 1)
                pool.wait_ge(pool_step, done(2))
                power = pool.tensor_tensor(rstd[:, :], var[:, 1, :], consts[:, 0, :], ALU.pow)
                if final:
                    power.then_inc(rstd_ready, 1)
                    return
                power.then_inc(pool_step, 1)
                pool.wait_ge(pool_step, done(3))
                pool.tensor_tensor(rstd_half[:, :], rstd[:, :], consts[:, 1, :], ALU.mult).then_inc(rstd_ready, 1)

            sections = ((A_Q, 9, ((8, 0),)), (I_Q, 5, ((4, 1),)), (B_Q, 10, ((8, 2), (9, 3))),
                        (C_Q, 8, ()), (C_K, 8, ()))
            with pool.Fori(0, LAYERS) as l:
                inverse_rms(l * 2 + 1, lambda n: l * POOL_PER_LAYER + n)
                for n, (col, heads, shared) in enumerate(sections):
                    chunks = 1 - (-(col + heads * HD - SHORT) // CW)
                    if n:
                        pool.wait_ge(rope_done, l * 5 + n)
                    pool.wait_ge(proj_ready, proj_no(l, 2 * chunks))
                    v = proj[:, :, col:col + heads * HD].rearrange("p m (h d) -> p m h d", d=HD)
                    t1 = rt1[:, 0:2 * heads * HD].rearrange("p (m h d) -> p m h d", m=MT, d=HD)
                    t2 = rt2[:, 0:2 * heads * HD].rearrange("p (m h d) -> p m h d", m=MT, d=HD)
                    cs = rope_sb[:, :, 0, :].unsqueeze(2).to_broadcast([P, MT, heads, HD])
                    sn = rope_sb[:, :, 1, :].unsqueeze(2)
                    half = HD // 2
                    pool.tensor_tensor(t1, v, cs, ALU.mult)
                    pool.tensor_tensor(t2[:, :, :, 0:half], v[:, :, :, half:HD],
                                       sn[:, :, :, 0:half].to_broadcast([P, MT, heads, half]), ALU.mult)
                    pool.tensor_tensor(t2[:, :, :, half:HD], v[:, :, :, 0:half],
                                       sn[:, :, :, half:HD].to_broadcast([P, MT, heads, half]),
                                       ALU.mult).then_inc(pool_step, 1)
                    pool.wait_ge(pool_step, l * POOL_PER_LAYER + (3 + n + 1))
                    for h, place in shared:
                        two = [P, MT, 2, HD]
                        pool.tensor_tensor(k_pair[:, place, :, :].rearrange("p m (t d) -> p m t d", t=2),
                                           t1[:, :, h, :].unsqueeze(2).to_broadcast(two),
                                           t2[:, :, h, :].unsqueeze(2).to_broadcast(two), ALU.add)
                    pool.tensor_tensor(v, t1, t2, ALU.add).then_inc(rope_done, 1)
                for r in range(6):
                    if r % 3 == 0:
                        continue
                    c = r // 3
                    for m in range(MT):
                        pool.wait_ge(part_ready, l * 12 + 2 * r + m + 1)
                        if r % 3 == 2:
                            pool.wait_ge(part_added, l * 8 + 4 * c + m + 1)
                        cols = merged[:, m, c * CW:(c + 1) * CW]
                        pool.tensor_tensor(cols, cols, part[:, m, :], ALU.add).then_inc(part_added, 1)
                inverse_rms(l * 2 + 2, lambda n: l * POOL_PER_LAYER + (8 + n))

                def square(chunk, first=False):
                    for m in range(MT):
                        pool.wait_ge(relu_ready, l * 2 * FFC + chunk * 2 + m + 1)
                        if not first:
                            pool.wait_ge(act_t, l * 2 * FFC + chunk * 2)
                        pool.tensor_tensor(up_sq[:, m, :], up_relu[:, m, :], up_relu[:, m, :],
                                           ALU.mult).then_inc(sq_ready, 1)

                square(0, first=True)
                square(1)
                with pool.Fori(0, MLP_ROUNDS) as i:
                    for a in range(2):
                        square(i * 2 + (2 + a))
            pool.wait_ge(gf_in, 16)
            pool.wait_ge(x_ready, LAYERS * 8 + 2)
            for m in range(MT):
                pool.tensor_tensor(normed[:, m, 0:CW], xs[:, m, 0:CW], gain_f[:, 0:CW],
                                   ALU.mult).then_inc(gained[0], 1)
            inverse_rms(2 * LAYERS + 1, lambda n: LAYERS * POOL_PER_LAYER + n, final=True)

        @block.tensor
        def _(pe):
            pe.wait_ge(ident_in, 16)
            pe.sem_inc(mm_done, 2 * RING)

            def unit(l, k, left_hi, left_lo, banks, first, last, it=None, free=None, pauses=None, left=None):
                slot, n, width = k % RING, 0, width_of(k, it)
                pe.wait_ge(lo_ready, unit_no(l, k, it) + 1 + RAW)
                for m in range(MT):
                    if free:
                        free(m)
                    for kt in range(KU):
                        if left and m == 0 and kt % 2 == 0:
                            left(kt // 2)
                        rows = slice(m * P, (m + 1) * P)
                        for p, (a, w) in enumerate(((left_hi, w_hi), (left_hi, w_lo), (left_lo, w_hi))):
                            if pauses and n % 4 == 0 and n // 4 in pauses:
                                pauses[n // 4]()
                            n += 1
                            ins = pe.matmul(bank[banks + m][:, 0:width], a[:, kt, rows],
                                            w[:, slot, kt, 0:width],
                                            start=first and kt == 0 and p == 0,
                                            stop=last and kt == KU - 1 and p == 2)
                    ins.then_inc(mm_done, 1)

            def rows_of(t, n):
                return t[:, KU * n:KU * (n + 1), :]

            def transpose_half(l, group, c, src):
                for b in range(2):
                    for a in range(2):
                        for m in range(MT):
                            kt = 4 * c + 2 * b + a
                            ins = pe.transpose(bank[(6, 4)[c] + b][:, a * SEQ + m * P:a * SEQ + (m + 1) * P],
                                               src[:, m, kt * P:(kt + 1) * P], ident[:, :])
                    ins.then_inc(half_t, 1)

            def t_job(l, kind, step):
                j = T_JOBS.index((kind, step))
                before = sum(1 for x in T_JOBS[:j] if x[0] == "o")
                b, p = STEPS[step]
                if j:
                    pe.wait_ge(t_taken, l * NT + j)
                if before:
                    pe.wait_ge(ot_lo, l * NO + before)
                if kind == "o":
                    pe.wait_ge(o_ready, l * NO + (step - 2) + 1)
                else:
                    pe.wait_ge(rope_done, l * 5 + {"i": 2, "b": 3, "c": 5, "a": 5}[b])
                for m in range(MT):
                    if kind == "q":
                        src = proj[:, m, Q_COL[b] + P * p:Q_COL[b] + P * (p + 1)]
                    elif kind == "o":
                        src = o_sb[:, step % 2, 1 - m, :]
                    else:
                        col, heads = key_of(step)
                        if heads == 2:
                            src = proj[:, m, col:col + P]
                        else:
                            src = k_pair[:, {A_K: 0, I_K: 1, B_K: 2, B_K + HD: 3}[col], m, :]
                    ins = pe.transpose(bank[6][:, m * P:(m + 1) * P], src, ident[:, :])
                ins.then_inc(t_done, 1)

            def scores(l, s):
                b, p = STEPS[s]
                q_job = T_JOBS.index(("q", s))
                jobs = [q_job] + [T_JOBS.index(("k", x)) for x in range(s + 1) if key_of(x)][-1:]
                pe.wait_ge(t_taken, l * NT + max(jobs) + 1)
                if s:
                    pe.wait_ge(exp_done, l * 4 * NS + 4 * s)
                if s == FIRST_A:
                    pe.wait_ge(chosen, l * 2 + 2)
                kb = k_t[:, KEY_JOB[s] % 2, :]
                if b != "i":
                    if s == 2:
                        pe.wait_ge(const_ready, CONSTS)
                    for j in range(2):
                        pe.matmul(bank[2 + j][:, 0:384], ident_neg[:, :],
                                  mask_b[:, {"c": 0, "b": 1, "a": 2}[b], :], start=True, stop=False)
                for m, keys, lo in ((1, 256, 0), (0, 128, 256)):
                    for j in range(2):
                        rows = slice(HD * j, HD * j + HD)
                        ins = pe.matmul(bank[2 + j][:, lo:lo + keys],
                                        q_t[rows, s % 2, m * P:(m + 1) * P], kb[rows, 0:keys],
                                        start=b == "i", stop=b == "i" or m == 0)
                        if m == 0:
                            ins.then_inc(s_done, 1)

            def transpose_probs(l, s):
                par = s % 2
                pe.wait_ge(exp_done, l * 4 * NS + 4 * s + 4)
                if s > 2:
                    pe.wait_ge(pt1_taken, l * NO + s - 2)
                    pe.wait_ge(pt0_taken, l * NO + s - 2)
                for n in range(6):
                    dst = bank[4][:, n * P:(n + 1) * P] if n < 4 else bank[5][:, (n - 4) * P:(n - 3) * P]
                    ins = pe.transpose(dst, prob[:, par, n * P:(n + 1) * P], ident[:, :])
                    if n in (3, 5):
                        ins.then_inc(pt_done, 1)

            def values(l, s):
                b, p = STEPS[s]
                pe.wait_ge(pt1_taken, l * NO + s - 1)
                pe.wait_ge(pt0_taken, l * NO + s - 1)
                if b == "c":
                    pe.wait_ge(proj_ready, proj_no(l, 2 * QKV_CHUNKS))
                if s > 2:
                    pe.wait_ge(o_ready, l * NO + s - 2)
                for n in range(4):
                    col = value_col(b, 2 * p + n % 2)
                    blocks = 2 if n < 2 else 1
                    for kb in range(blocks):
                        at = 3 * (n % 2) + (kb if n < 2 else 2)
                        ins = pe.matmul(bank[7][:, n * HD:(n + 1) * HD], prob_t[:, at * P:(at + 1) * P],
                                        proj[:, kb, col:col + HD], start=kb == 0, stop=kb == blocks - 1)
                ins.then_inc(pv_done, 1)

            with pe.Fori(0, LAYERS) as l:
                pe.wait_ge(x_ready, l * 8 + 2)
                transpose_half(l, 0, 0, xs)
                for r in range(2):
                    pauses = {}
                    if r == 0:
                        def x_half():
                            pe.wait_ge(x_ready, l * 8 + 4)
                            transpose_half(l, 0, 1, xs)
                        pauses[4] = x_half

                    def left(b):
                        pe.wait_ge(half_lo, l * 12 + 2 * r + b + 1)
                    unit(l, r, rows_of(h_hi, r), rows_of(h_lo, r), 0, r == 0, r == 1,
                         pauses=pauses, left=left)
                with pe.Fori(0, 2) as i:
                    for j in range(RING):
                        banks = 2 - 2 * (j // 2)

                        def free(m, j=j):
                            if j == 0:
                                pe.wait_ge(proj_ready, proj_no(l, 0) + i * 4)
                            if j == 2:
                                pe.wait_ge(proj_ready, proj_no(l, m + 1) + i * 4)
                        unit(l, 2 + j, rows_of(h_hi, j % 2), rows_of(h_lo, j % 2), banks, j % 2 == 0, j % 2 == 1,
                             it=i, free=free)
                for u in range(K_OUT - K_STRAIGHT):
                    k = K_STRAIGHT + u
                    pauses = {}
                    if 1 <= u <= NS:
                        pauses[0] = lambda: scores(l, u - 1)
                    if u < NS:
                        pauses[1] = lambda: t_job(l, "q", u)
                        if key_of(u):
                            pauses[3] = lambda: t_job(l, "k", u)
                    if 4 <= u <= NS + 1:
                        pauses[2] = lambda: transpose_probs(l, u - 2)
                        pauses[4] = lambda: values(l, u - 2)
                    if 5 <= u <= NS + 2:
                        pauses[5] = lambda: t_job(l, "o", u - 3)
                    if k < K_BRANCH:
                        e, r = k // 2, k % 2

                        def free(m):
                            if r == 0:
                                pe.wait_ge(proj_ready, proj_no(l, 2 * (e - 1) + m + 1))
                        unit(l, k, rows_of(h_hi, r), rows_of(h_lo, r), 0, r == 0, r == 1, free=free, pauses=pauses)
                        continue
                    r = k - K_BRANCH
                    b = BRANCH_INDEX[BRANCHES[r % 3]]
                    if r == 1:
                        pe.wait_ge(exp_done, (l + 1) * (4 * NS))
                    if r == 2:
                        pe.wait_ge(ot_lo, (l + 1) * NO)
                    elif r < 2:
                        pe.wait_ge(ot_lo, l * NO + 4 * (r + 1))

                    def free(m):
                        if r == 0:
                            pe.wait_ge(proj_ready, proj_no(l, 2 * CHUNKS - 1 + m))
                        if r >= 2:
                            pe.wait_ge(part_ready, l * 12 + 2 * (r - 2) + m + 1)
                    if r == 4:
                        def merged_half():
                            pe.wait_ge(part_added, l * 8 + 4)
                            transpose_half(l, 1, 0, merged)
                        pauses[3] = merged_half
                    unit(l, k, rows_of(br_hi, b), rows_of(br_lo, b), 2 * (r % 2), True, True, free=free,
                         pauses=pauses)
                for r in range(4):
                    pauses = {}
                    if r == 1:
                        def merged_half():
                            pe.wait_ge(part_added, l * 8 + 8)
                            transpose_half(l, 1, 1, merged)
                        pauses[2] = merged_half
                    if r == 3:
                        def x_half():
                            pe.wait_ge(x_ready, l * 8 + 6)
                            transpose_half(l, 2, 0, xs)
                        pauses[2] = x_half

                    def free(m):
                        if r < 2:
                            pe.wait_ge(part_ready, l * 12 + 8 + 2 * r + m + 1)

                    def left(b):
                        if r % 2 == 0:
                            pe.wait_ge(half_lo, l * 12 + 4 + r + b + 1)
                    unit(l, K_OUT + r, rows_of(h_hi, r // 2), rows_of(h_lo, r // 2), 2 * (r % 2), r < 2, r >= 2,
                         free=free, pauses=pauses, left=left)
                def up(k, chunk, it=None, pause=None, first_chunk=False):
                    for r in range(2):
                        pauses = {}
                        if first_chunk and r == 0:
                            def x_half():
                                pe.wait_ge(x_ready, l * 8 + 8)
                                transpose_half(l, 2, 1, xs)
                            pauses[3] = x_half
                        if r == 1 and pause:
                            pauses[0] = pause

                        def free(m):
                            if r == 0 and not first_chunk:
                                pe.wait_ge(relu_ready, l * 2 * FFC + chunk * 2)

                        def left(b):
                            if first_chunk:
                                pe.wait_ge(half_lo, l * 12 + 8 + 2 * r + b + 1)
                        unit(l, k + r, rows_of(h_hi, r), rows_of(h_lo, r), 0, r == 0, r == 1, it=it, free=free,
                             pauses=pauses, left=left)

                def transpose_hidden(chunk):
                    pe.wait_ge(sq_ready, l * 2 * FFC + chunk * 2 + 2)
                    for b in range(2):
                        for a in range(2):
                            for m in range(MT):
                                kt = 2 * b + a
                                ins = pe.transpose(bank[6 + b][:, a * SEQ + m * P:a * SEQ + (m + 1) * P],
                                                   up_sq[:, m, kt * P:(kt + 1) * P], ident[:, :])
                        ins.then_inc(act_t, 1)

                def down(k, chunk, parity, it=None, last=False):
                    for r in range(2):
                        def left(b):
                            if r == 0:
                                pe.wait_ge(act_t_lo, l * 2 * FFC + chunk * 2 + b + 1)
                        pauses = {}
                        if r == 1 and not last:
                            pauses[0] = lambda: transpose_hidden(chunk + 1)
                        unit(l, k + r, act_hi[parity], act_lo[parity], 2 + 2 * r, False, last, it=it,
                             pauses=pauses, left=left)

                up(K_UP0, 0, first_chunk=True)
                pe.wait_ge(zero_ready, 1)
                pe.wait_ge(const_ready, CONSTS)
                for n in range(2, 6):
                    pe.matmul(bank[n][:, :], ident_neg[:, :], zeros[:, :], start=True, stop=False)
                up(K_UP1, 1, pause=lambda: transpose_hidden(0))
                down(K_UP1 + 2, 0, 0)
                with pe.Fori(0, MLP_ROUNDS) as i:
                    for a in range(2):
                        up(K_LOOP + RING * a, i * 2 + (2 + a), it=i * 2)
                        down(K_LOOP + RING * a + 2, i * 2 + (1 + a), 1 - a, it=i * 2)
                down(K_DOWN7, FFC - 1, (FFC - 1) % 2, last=True)


def rotation_table():
    import numpy as np
    inv = 1.0 / (np.float32(10000.0) ** (np.arange(0, HD, 2, dtype=np.float32) / np.float32(HD)))
    angle = np.arange(SEQ, dtype=np.float32)[:, None] * inv.astype(np.float32)[None, :]
    c, s = np.cos(angle), np.sin(angle)
    table = np.stack([np.concatenate([c, c], 1), np.concatenate([-s, s], 1)], 1)
    return np.ascontiguousarray(table.reshape(MT, P, 2, HD).transpose(1, 0, 2, 3).astype(np.float32))


def mask_table():
    import numpy as np
    row, key = np.arange(P)[:, None], np.arange(SEQ)[None, :]
    table = np.zeros((P, 2, 384), np.float32)
    for at, m, keys in ((0, 1, 256), (256, 0, 128)):
        diff = (row + m * P) - key[:, :keys]
        table[:, 0, at:at + keys] = diff < 0
        table[:, 1, at:at + keys] = (diff < 0) | (diff >= 128)
    return table


def kernel(x, norm1, w_in, sinks, w_branch, w_out, norm2, w_ff1, w_ff2, norm_f):
    import numpy as np
    import concourse.bacc as bacc
    from concourse.bass_utils import run_bass_kernel_spmd

    def features_on_rows(a):
        return a.reshape(LAYERS, KT, P).transpose(2, 0, 1).reshape(P, LAYERS * KT)

    nc = bacc.Bacc("TRN2", target_bir_lowering=False, num_devices=1)
    given = {"x": x, "norm1": features_on_rows(np.asarray(norm1)), "w_in": w_in, "sinks": sinks, "w_branch": w_branch, "w_out": w_out,
             "norm2": features_on_rows(np.asarray(norm2)), "w_ff1": w_ff1, "w_ff2": w_ff2, "norm_f": norm_f,
             "rope": rotation_table(), "masks": mask_table(), "identity": np.eye(P, dtype=np.float32)}
    arrays = {f"in_{n}": np.ascontiguousarray(a) for n, a in given.items()}
    aps = [nc.dram_tensor(n, a.shape, mybir.dt.from_np(a.dtype), kind="ExternalInput").ap()
           for n, a in arrays.items()]
    out = nc.dram_tensor("out_0", (1, SEQ, D), F32, kind="ExternalOutput").ap()
    program(nc, *aps, out)
    result = run_bass_kernel_spmd(nc, [arrays], core_ids=[0])
    return result.results[0]["out_0"]
```

```python
from contextlib import ExitStack

import concourse.bass as bass
from concourse import mybir

F32 = mybir.dt.float32
F32R = mybir.dt.float32r
BF16 = mybir.dt.bfloat16
ALU = mybir.AluOpType
ACT = mybir.ActivationFunctionType
AX = mybir.AxisListType

P = 128
SEQ = 256
MT = SEQ // P
D = 1024
KT = D // P
HD = 64
DFF = 4096
LAYERS = 2
EPS = 1e-6
QKV = 3268
GATES = 3 * D
CW = 512
KU = 4
SHORT = QKV % CW
QKV_CHUNKS = 1 + QKV // CW
CHUNKS = QKV_CHUNKS + GATES // CW
RING = 4
RAW = 2
WARM_UP = 8
FFC = DFF // CW

K_STRAIGHT = 10
K_GATES = 2 * QKV_CHUNKS
K_BRANCH = K_GATES + 2 * (GATES // CW)
K_OUT = K_BRANCH + 6
K_UP0 = K_OUT + 4
K_UP1 = K_UP0 + 2
K_LOOP = K_UP1 + RING
MLP_ROUNDS = (FFC - 2) // 2
K_DOWN7 = K_UP1 + RING * (FFC - 1)
UNITS = K_DOWN7 + 2
assert UNITS % RING == 0 and FFC % 2 == 0 and K_DOWN7 == K_LOOP + 2 * RING * MLP_ROUNDS

A_Q, A_K, A_V = 0, 512, 576
I_Q, I_K, I_W = 640, 896, 960
B_Q, B_K, B_V = 964, 1476, 1604
C_Q, C_K, C_V = 1732, 2244, 2756

SCALE = HD ** -0.5
IDX_SCALE = (64 ** -0.5) * (4 ** -0.5)
TOPK = SEQ // 4
ROUNDS = TOPK // 8
TAKEN = -3.0e38
MASKED = -1.0e30

STEPS = [("i", 0), ("i", 1)] + [(b, p) for b in "bca" for p in range(4)]
NS = len(STEPS)
Q_COL = {"a": A_Q, "i": I_Q, "b": B_Q, "c": C_Q}
BRANCHES = "bca"
BRANCH_INDEX = {"a": 0, "b": 1, "c": 2}
FIRST_A = STEPS.index(("a", 0))


def key_of(step):
    b, p = STEPS[step]
    if b == "i":
        return (I_K, 1) if p == 0 else None
    if b == "a":
        return (A_K, 1) if p == 0 else None
    if b == "b":
        return (B_K + HD * (p // 2), 1) if p % 2 == 0 else None
    return C_K + P * p, 2


KEY_JOB = {}
for _s in range(NS):
    KEY_JOB[_s] = (KEY_JOB[_s - 1] if _s else -1) + (key_of(_s) is not None)

T_JOBS = []
for _u in range(NS):
    T_JOBS.append(("q", _u))
    if key_of(_u):
        T_JOBS.append(("k", _u))
NT = len(T_JOBS)
NO = NS - 2


def width_of(k, it):
    return SHORT if it is None and k < 2 else CW


def value_col(branch, head):
    return {"a": A_V, "b": B_V + HD * (head // 4), "c": C_V + HD * head}[branch]


def program(nc, x, norm1, w_in, sinks, w_branch, w_out, norm2, w_ff1, w_ff2, norm_f, rope, masks,
            identity, out):
    win_v = w_in.rearrange("l (k p) n -> p (l k) n", p=P)
    wbr_v = w_branch.rearrange("l b (k p) n -> p (l b k) n", p=P)
    wout_v = w_out.rearrange("l (k p) n -> p (l k) n", p=P)
    wup_v = w_ff1.rearrange("l (k p) n -> p (l k) n", p=P)
    wdown_v = w_ff2.rearrange("l (k p) n -> p (l k) n", p=P)
    x_v = x.rearrange("b (m p) d -> p (b m) d", p=P)
    out_v = out.rearrange("b (m p) d -> p (b m) d", p=P)

    with ExitStack() as ctx:
        def sb(name, shape, dt=F32):
            return ctx.enter_context(nc.sbuf_tensor(name, shape, dt))

        def sem(name):
            return ctx.enter_context(nc.semaphore(name))

        bank = [ctx.enter_context(nc.psum_tensor(f"bank{i}", [P, 512], F32)) for i in range(8)]

        raw = sb("raw", [P, RAW, KU, CW])
        raw_short = sb("raw_short", [P, 2, KU, SHORT])
        w_hi = sb("w_hi", [P, RING, KU, CW], F32R)
        w_lo = sb("w_lo", [P, RING, KU, CW], F32R)
        xs = sb("xs", [P, MT, D])
        h_hi = sb("h_hi", [P, KT, SEQ], F32R)
        h_lo = sb("h_lo", [P, KT, SEQ], F32R)
        br_hi = sb("br_hi", [P, 12, SEQ], F32R)
        br_lo = sb("br_lo", [P, 12, SEQ], F32R)
        act_hi = [br_hi[:, KU * n:KU * (n + 1), :] for n in range(2)]
        act_lo = [br_lo[:, KU * n:KU * (n + 1), :] for n in range(2)]
        proj = sb("proj", [P, MT, QKV])
        merged = proj[:, :, 0:D]
        gate = sb("gate", [P, MT, GATES])
        gate_flat = gate[:, :, :].rearrange("p m n -> p (m n)")
        rt1 = gate_flat[:, 0:1280]
        rt2 = gate_flat[:, 1280:2560]
        relu_dots = gate_flat[:, 2560:2560 + 4 * 384].rearrange("p (h n) -> p h n", h=4)
        score = gate_flat[:, 5632:6016]
        picked = gate_flat[:, 5120:5504]
        up_relu = gate_flat[:, 0:1024].rearrange("p (m n) -> p m n", m=MT)
        up_sq = gate_flat[:, 1024:2048].rearrange("p (m n) -> p m n", m=MT)
        squares = gate_flat[:, 2048:4096].rearrange("p (m n) -> p m n", m=MT)
        gain_f = gate_flat[:, 4096:5120]
        normed = gate_flat[:, 0:2048].rearrange("p (m n) -> p m n", m=MT)
        q_t = sb("q_t", [P, 2, SEQ])
        k_t = sb("k_t", [P, 2, SEQ])
        k_pair = sb("k_pair", [P, 4, MT, P])
        prob = sb("prob", [P, 2, 768])
        part = prob[:, :, :].rearrange("p a n -> p (a n)")[:, 0:1024].rearrange("p (m n) -> p m n", m=MT)
        prob_t = sb("prob_t", [P, 768])
        rope_sb = sb("rope_sb", [P, MT, 2, HD])
        mask_b = sb("mask_b", [P, 3, 384], BF16)
        table_out = sb("table_out", [P, 1])
        ident = sb("ident", [P, P])
        ident_neg = sb("ident_neg", [P, P], BF16)
        zeros = sb("zeros", [P, CW], BF16)
        top8 = sb("top8", [P, 2, 8])
        gain = sb("gain", [P, 2, KT])
        sink_neg = sb("sink_neg", [P, 8])
        sink_raw = sb("sink_raw", [P, 8])
        consts = sb("consts", [P, 3, MT])
        ssq = sb("ssq", [P, 2, MT])
        var = sb("var", [P, 2, MT])
        rstd = sb("rstd", [P, MT])
        rstd_half = sb("rstd_half", [P, MT])
        row_max = sb("row_max", [P, 2, 4])
        neg_max = sb("neg_max", [P, 2, 4])
        row_sum = sb("row_sum", [P, 2, 4])
        sink_arg = sb("sink_arg", [P, 2, 4])
        sink_exp = sb("sink_exp", [P, 2, 4])
        row_inv = sb("row_inv", [P, 2, 4])

        raw_in = [sem(f"raw_in{i}") for i in range(RAW)]
        short_in = [sem(f"short_in{i}") for i in range(2)]
        x_in = [sem(f"x_in{c}") for c in range(2)]
        ident_in, rope_in, mask_in, small_in, out_sent, gf_in = (sem(n) for n in (
            "ident_in", "rope_in", "mask_in", "small_in", "out_sent", "gf_in"))
        hi_ready = sem("hi_ready")
        lo_ready = sem("lo_ready")
        mm_done = sem("mm_done")
        x_ready = sem("x_ready")
        const_ready = sem("const_ready")
        consts_set = sem("consts_set")
        zero_ready = sem("zero_ready")
        half_t = sem("half_t")
        half_hi = sem("half_hi")
        half_lo = sem("half_lo")
        ssq_ready = sem("ssq_ready")
        rstd_ready = sem("rstd_ready")
        proj_ready = sem("proj_ready")
        rope_done = sem("rope_done")
        t_done = sem("t_done")
        t_taken = sem("t_taken")
        s_done = sem("s_done")
        neg_ready = sem("neg_ready")
        exp_done = sem("exp_done")
        sink_arg_ready = sem("sink_arg_ready")
        sink_exp_ready = sem("sink_exp_ready")
        pt_done = sem("pt_done")
        pt1_taken = sem("pt1_taken")
        pt0_taken = sem("pt0_taken")
        prob_ready = sem("prob_ready")
        pv_done = sem("pv_done")
        o_hi = sem("o_hi")
        o_lo = sem("o_lo")
        chosen = sem("chosen")
        part_ready = sem("part_ready")
        part_added = sem("part_added")
        relu_ready = sem("relu_ready")
        sq_ready = sem("sq_ready")
        act_t = sem("act_t")
        act_t_hi = sem("act_t_hi")
        act_t_lo = sem("act_t_lo")
        dve_step = sem("dve_step")
        pool_step = sem("pool_step")
        gained = sem("gained")
        last_gained = sem("last_gained")
        y_ready = sem("y_ready")
        y_ready_act = sem("y_ready_act")
        table_ready = sem("table_ready")
        wait_passed = sem("wait_passed")

        def proj_no(l, n):
            return l * (2 * CHUNKS) + (n + 1)

        def raw_of(k, it):
            if width_of(k, it) == SHORT:
                return raw_short[:, k, :, :]
            return raw[:, k % RAW, :, :]

        def unit_no(l, k, it=None):
            n = l * UNITS + k
            return n if it is None else n + it * RING

        def half_no(l, k, m, it=None):
            n = l * (2 * UNITS) + (2 * k + m + 1 + 2 * RING)
            return n if it is None else n + it * (2 * RING)

        class Count:
            def __init__(self, per_layer):
                self.per_layer, self.n = per_layer, 0

            def one_more(self):
                self.n += 1
                return 1

            def value(self, l, n=None):
                return l * self.per_layer + (self.n if n is None else n)

        DVE_PER_LAYER = 1 + 2 * 4 + 1 + 4 * ROUNDS + 4 * NO + 4 + NO
        POOL_PER_LAYER = 2 * 3 + 5

        block = ctx.enter_context(nc.Block())

        @block.sync
        def _(sp):
            sp.sem_inc(lo_ready, RAW)
            sp.dma_start(xs[:, :, 0:CW], x_v[:, :, 0:CW]).then_inc(x_in[0], 16)

            def load(l, k, source, it=None):
                sp.wait_ge(lo_ready, unit_no(l, k - 2 if it is None and k < 4 else k, it) + 1)
                sp.dma_start(raw[:, k % RAW, :, :], source).then_inc(raw_in[k % RAW], 16)

            with sp.Fori(0, LAYERS) as l:
                sp.dma_start(gain[:, 0, :], norm1[:, bass.ds(l * KT, KT)]).then_inc(small_in, 16)
                sp.dma_start(gain[:, 1, :], norm2[:, bass.ds(l * KT, KT)]).then_inc(small_in, 16)
                sp.dma_start(sink_raw[:, :], sinks[bass.ds(l, 1), :].to_broadcast([P, 8])).then_inc(small_in, 16)
                for r in range(2):
                    sp.dma_start(raw_of(r, None), win_v[:, bass.ds(l * KT + r * KU, KU), 0:SHORT]).then_inc(
                        short_in[r], 16)
                sp.wait_ge(short_in[0], (l + 1) * 16)

                def load_in(k, it=None):
                    col = SHORT + (k // 2 - 1) * CW
                    load(l, k, win_v[:, bass.ds(l * KT + (k % 2) * KU, KU),
                                     bass.ds(col if it is None else it * (2 * CW) + col, CW)], it=it)

                for k in range(2, 2 + RING):
                    load_in(k)
                with sp.Fori(0, (K_BRANCH - 2) // RING - 1) as i:
                    for j in range(RING):
                        load_in(2 + RING + j, it=i)
                for r in range(6):
                    c, b = r // 3, BRANCH_INDEX[BRANCHES[r % 3]]
                    load(l, K_BRANCH + r, wbr_v[:, bass.ds(l * 12 + b * KU, KU), c * CW:(c + 1) * CW])
                for r in range(4):
                    load(l, K_OUT + r, wout_v[:, bass.ds(l * KT + (r // 2) * KU, KU),
                                              (r % 2) * CW:(r % 2 + 1) * CW])
                for r in range(2):
                    load(l, K_UP0 + r, wup_v[:, bass.ds(l * KT + r * KU, KU), 0:CW])
                with sp.Fori(0, FFC - 1) as i:
                    for r in range(2):
                        load(l, K_UP1 + r, wup_v[:, bass.ds(l * KT + r * KU, KU), bass.ds((i + 1) * CW, CW)],
                             it=i)
                    for r in range(2):
                        load(l, K_UP1 + 2 + r, wdown_v[:, bass.ds(l * (DFF // P) + i * KU, KU),
                                                        r * CW:(r + 1) * CW], it=i)
                for r in range(2):
                    load(l, K_DOWN7 + r, wdown_v[:, bass.ds(l * (DFF // P) + (FFC - 1) * KU, KU),
                                                 r * CW:(r + 1) * CW])
            sp.wait_ge(act_t, 2 * FFC * LAYERS)
            sp.dma_start(gain_f, norm_f.rearrange("(o n) -> o n", o=1).to_broadcast([P, D])).then_inc(gf_in, 16)
            sp.wait_ge(y_ready, 2)
            sp.dma_start(out_v[:, 0, :], normed[:, 0, :]).then_inc(out_sent, 16)
            sp.wait_ge(y_ready, 3)
            sp.dma_start(out_v[:, 1, CW:D], normed[:, 1, CW:D]).then_inc(out_sent, 16)
            sp.wait_ge(out_sent, 16 * 3)

        @block.scalar
        def _(act):
            act.sem_inc(proj_ready, 1)
            act.dma_start(ident[:, :], identity).then_inc(ident_in, 16)
            act.wait_ge(zero_ready, 1)
            act.activation(table_out[:, :], zeros[:, 0:1], ACT.Exp).then_inc(table_ready, 1)
            act.wait_ge(x_in[0], 16)
            act.dma_start(xs[:, :, CW:D], x_v[:, :, CW:D]).then_inc(x_in[1], 16)

            def high(l, k, it=None):
                width = width_of(k, it)
                if width == SHORT:
                    act.wait_ge(short_in[k], (l + 1) * 16)
                else:
                    n = l * (UNITS // RAW - 1) + k // RAW
                    if it is not None:
                        n = n + it * (RING // RAW)
                    act.wait_ge(raw_in[k % RAW], n * 16)
                act.wait_ge(mm_done, half_no(l, k - RING, 1, it))
                act.activation(w_hi[:, k % RING, :, 0:width], raw_of(k, it),
                               ACT.Copy).then_inc(hi_ready, 1)

            def half_high(l, group, c, gains):
                for b in range(2):
                    act.wait_ge(half_t, l * 12 + (4 * group + 2 * c + b + 1))
                    src = bank[(6, 4)[c] + b]
                    kt = 4 * c + 2 * b
                    if gains is None:
                        act.activation(h_hi[:, kt:kt + 2, :], src[:, :].rearrange("p (a n) -> p a n", a=2),
                                       ACT.Copy, scale=0.5).then_inc(half_hi, 1)
                    else:
                        act.activation(h_hi[:, kt, :], src[:, 0:SEQ], ACT.Identity, bias=0.0,
                                       scale=gain[:, gains, kt:kt + 1])
                        act.activation(h_hi[:, kt + 1, :], src[:, SEQ:512], ACT.Identity, bias=0.0,
                                       scale=gain[:, gains, kt + 1:kt + 2]).then_inc(half_hi, 1)

            def sum_squares(l, which):
                for c in range(2):
                    for m in range(MT):
                        act.wait_ge(x_ready, l * 8 + 4 * which + 2 * c + m + 1)
                        act.activation(squares[:, m, c * CW:(c + 1) * CW], xs[:, m, c * CW:(c + 1) * CW],
                                       ACT.Square, scale=D ** -0.5, accum_out=ssq[:, c, m:m + 1]).then_inc(ssq_ready, 1)

            def take_proj(l, e, k, m, it=None):
                act.wait_ge(mm_done, half_no(l, k, m, it))
                src = bank[(2 * (e % 2) if e < 5 else 0) + m]
                if e < QKV_CHUNKS:
                    width = width_of(k, it)
                    col = e * CW - (CW - SHORT if e else 0)
                    act.activation(proj[:, m, col:col + width], src[:, 0:width], ACT.Identity, bias=0.0,
                                   scale=rstd[:, m:m + 1]).then_inc(proj_ready, 1)
                else:
                    g = e - QKV_CHUNKS
                    act.activation(gate[:, m, g * CW:(g + 1) * CW], src[:, :], ACT.Tanh, bias=0.0,
                                   scale=rstd_half[:, m:m + 1]).then_inc(proj_ready, 1)

            def take_t(l, kind, step):
                j = T_JOBS.index((kind, step))
                act.wait_ge(t_done, l * NT + j + 1)
                src = bank[6][:, 0:SEQ]
                if kind == "q":
                    act.activation(q_t[:, step % 2, :], src, ACT.Copy).then_inc(t_taken, 1)
                else:
                    act.activation(k_t[:, KEY_JOB[step] % 2, :], src, ACT.Copy).then_inc(t_taken, 1)

            def out_high(l, s):
                b, p = STEPS[s]
                act.wait_ge(pv_done, l * NO + (s - 2) + 1)
                act.activation(br_hi[:, 4 * BRANCH_INDEX[b] + p, :], bank[7][:, 0:SEQ],
                               ACT.Copy).then_inc(o_hi, 1)

            def exponentials(l, s):
                par = s % 2
                act.wait_ge(s_done, l * 2 * NS + 2 * s + 2)
                if s < 2:
                    for j in range(2):
                        act.activation(relu_dots[:, 2 * s + j, :], bank[2 + j][:, 0:384],
                                       ACT.Relu, scale=IDX_SCALE).then_inc(exp_done, 2)
                    return
                act.wait_ge(neg_ready, l * NO + (s - 2) + 1)
                for n in range(4):
                    lo, w = (0, 256) if n < 2 else (256, 128)
                    act.activation(prob[:, par, 384 * (n % 2) + lo:384 * (n % 2) + lo + w],
                                   bank[2 + n % 2][:, lo:lo + w], ACT.Exp, bias=neg_max[:, par, n:n + 1],
                                   scale=SCALE, accum_out=row_sum[:, par, n:n + 1]).then_inc(exp_done, 1)
                if STEPS[s][0] == "b":
                    act.wait_ge(sink_arg_ready, l * 4 + (s - 2) + 1)
                    act.activation(sink_exp[:, par, :], sink_arg[:, par, :], ACT.Exp).then_inc(sink_exp_ready, 1)

            def take_probs(l, s):
                act.wait_ge(pt_done, l * 2 * NO + 2 * (s - 2) + 1)
                act.activation(prob_t[:, 0:512], bank[4][:, :], ACT.Copy).then_inc(pt1_taken, 1)

            def hidden_high(l, chunk, parity):
                for b in range(2):
                    act.wait_ge(act_t, l * 2 * FFC + chunk * 2 + b + 1)
                    act.activation(act_hi[parity][:, 2 * b:2 * b + 2, :],
                                   bank[6 + b][:, :].rearrange("p (a n) -> p a n", a=2),
                                   ACT.Copy).then_inc(act_t_hi, 1)

            def take_up(l, k, chunk, it=None, first_chunk=False, banks=0):
                for m in range(MT):
                    act.wait_ge(mm_done, half_no(l, k + 1, m, it))
                    if not first_chunk:
                        act.wait_ge(sq_ready, l * 2 * FFC + chunk * 2)
                    act.activation(up_relu[:, m, :], bank[banks + m][:, :], ACT.Relu,
                                   scale=rstd[:, m:m + 1]).then_inc(relu_ready, 1)

            with act.Fori(0, LAYERS) as l:
                high(l, 0)
                act.wait_ge(small_in, l * 48 + 48)
                half_high(l, 0, 0, 0)
                high(l, 1)
                half_high(l, 0, 1, 0)
                high(l, 2)
                sum_squares(l, 0)
                high(l, 3)
                act.wait_ge(rstd_ready, l * 2 + 1)
                for m in range(MT):
                    take_proj(l, 0, 1, m)
                with act.Fori(0, 2) as i:
                    for j in range(2):
                        high(l, 4 + 2 * j, it=i)
                        high(l, 5 + 2 * j, it=i)
                        for m in range(MT):
                            act.wait_ge(mm_done, half_no(l, 3 + 2 * j, m, i))
                            act.activation(proj[:, m, bass.ds(i * (2 * CW) + (SHORT + j * CW), CW)],
                                           bank[2 * (1 - j) + m][:, :], ACT.Identity, bias=0.0,
                                           scale=rstd[:, m:m + 1]).then_inc(proj_ready, 1)
                for u in range(K_OUT - K_STRAIGHT):
                    k = K_STRAIGHT + u
                    high(l, k + 2)
                    if u < NS:
                        take_t(l, "q", u)
                    if 1 <= u <= NS:
                        exponentials(l, u - 1)
                    if 4 <= u <= NS + 1:
                        take_probs(l, u - 2)
                    last = k < K_BRANCH and k % 2 == 1
                    e = k // 2
                    if k == K_GATES + 1:
                        act.wait_ge(rope_done, l * 5 + 5)
                        act.wait_ge(chosen, l * 2 + 1)
                    if k == K_GATES + 9:
                        act.wait_ge(chosen, l * 2 + 2)
                    if last:
                        take_proj(l, e, k, 0)
                    if u < NS and key_of(u):
                        take_t(l, "k", u)
                    if last:
                        take_proj(l, e, k, 1)
                    if 4 <= u <= NS + 1:
                        out_high(l, u - 2)
                    if k == K_BRANCH + 4:
                        half_high(l, 1, 0, None)
                high(l, K_OUT + 2)
                high(l, K_OUT + 3)
                half_high(l, 1, 1, None)
                high(l, K_OUT + 4)
                high(l, K_OUT + 5)
                half_high(l, 2, 0, 1)
                half_high(l, 2, 1, 1)
                sum_squares(l, 1)
                high(l, K_UP1)
                high(l, K_UP1 + 1)
                act.wait_ge(rstd_ready, l * 2 + 2)
                take_up(l, K_UP0, 0, first_chunk=True)
                high(l, K_UP1 + 2)
                hidden_high(l, 0, 0)
                high(l, K_UP1 + 3)
                take_up(l, K_UP1, 1, banks=2)
                high(l, K_UP1 + 4)
                hidden_high(l, 1, 1)
                high(l, K_UP1 + 5)
                with act.Fori(0, MLP_ROUNDS) as i:
                    for a in range(2):
                        k = K_LOOP + RING * a
                        high(l, k + 2, it=i * 2)
                        high(l, k + 3, it=i * 2)
                        take_up(l, k, i * 2 + (2 + a), it=i * 2)
                        high(l, k + 4, it=i * 2)
                        hidden_high(l, i * 2 + (2 + a), a)
                        high(l, k + 5, it=i * 2)
            sum_squares(LAYERS - 1, 2)
            act.wait_ge(gained, 2)
            act.wait_ge(rstd_ready, 2 * LAYERS + 2)
            cols = normed[:, 1, 0:CW]
            act.activation(cols, cols, ACT.Identity, bias=0.0, scale=rstd[:, 1:2]).then_inc(y_ready_act, 1)
            act.wait_ge(y_ready_act, 1)
            act.dma_start(out_v[:, 1, 0:CW], cols).then_inc(out_sent, 16)

        @block.vector
        def _(dve):
            dve.memset(zeros[:, :], 0.0).then_inc(zero_ready, 1)
            dve.wait_ge(x_in[0], 16)
            dve.sem_inc(x_ready, 2)

            def low(l, k, it=None):
                width = width_of(k, it)
                dve.wait_ge(hi_ready, unit_no(l, k, it) + 1)
                dve.tensor_tensor(w_lo[:, k % RING, :, 0:width], raw_of(k, it),
                                  w_hi[:, k % RING, :, 0:width].bitcast(F32),
                                  ALU.subtract).then_inc(lo_ready, 1)

            def half_low(l, group, c, gains):
                for b in range(2):
                    dve.wait_ge(half_hi, l * 12 + (4 * group + 2 * c + b + 1))
                    src = bank[(6, 4)[c] + b]
                    kt = 4 * c + 2 * b
                    if gains is None:
                        dve.scalar_tensor_tensor(
                            h_lo[:, kt:kt + 2, :], src[:, :].rearrange("p (a n) -> p a n", a=2), 0.5,
                            h_hi[:, kt:kt + 2, :].bitcast(F32), ALU.mult, ALU.subtract).then_inc(half_lo, 1)
                        continue
                    for a in range(2):
                        ins = dve.scalar_tensor_tensor(
                            h_lo[:, kt + a, :], src[:, a * SEQ:(a + 1) * SEQ], gain[:, gains, kt + a:kt + a + 1],
                            h_hi[:, kt + a, :].bitcast(F32), ALU.mult, ALU.subtract)
                    ins.then_inc(half_lo, 1)

            def add_to_x(l, c, k, banks):
                for m in range(MT):
                    dve.wait_ge(mm_done, half_no(l, k, m))
                    cols = xs[:, m, c * CW:(c + 1) * CW]
                    dve.tensor_tensor(cols, cols, bank[banks + m][:, :], ALU.add).then_inc(x_ready, 1)

            def maxima(l, own, s):
                par, b = s % 2, STEPS[s][0]
                dve.wait_ge(s_done, l * 2 * NS + 2 * s + 2)
                for n in range(4):
                    lo, w = (0, 256) if n < 2 else (256, 128)
                    dve.tensor_reduce(row_max[:, par, n:n + 1], bank[2 + n % 2][:, lo:lo + w],
                                      AX.X, ALU.max).then_inc(dve_step, own.one_more())
                dve.wait_ge(dve_step, own.value(l))
                if b != "b":
                    dve.tensor_scalar(neg_max[:, par, :], row_max[:, par, :], -SCALE, None,
                                      ALU.mult).then_inc(neg_ready, 1)
                    return
                p = STEPS[s][1]
                sk = sink_neg[:, 2 * p:2 * p + 2].unsqueeze(1).to_broadcast([P, 2, 2])
                dve.scalar_tensor_tensor(
                    neg_max[:, par, :].rearrange("p (m h) -> p m h", m=2),
                    row_max[:, par, :].rearrange("p (m h) -> p m h", m=2), -SCALE, sk,
                    ALU.mult, ALU.min).then_inc(neg_ready, 1)
                dve.wait_ge(neg_ready, l * NO + (s - 2) + 1)
                dve.tensor_tensor(sink_arg[:, par, :].rearrange("p (m h) -> p m h", m=2),
                                  neg_max[:, par, :].rearrange("p (m h) -> p m h", m=2), sk,
                                  ALU.subtract).then_inc(sink_arg_ready, 1)

            def take_probs(l, s):
                dve.wait_ge(pt_done, l * 2 * NO + 2 * (s - 2) + 2)
                dve.tensor_copy(prob_t[:, 512:768], bank[5][:, 0:256]).then_inc(pt0_taken, 1)

            def normalise(l, own, s):
                par = s % 2
                dve.wait_ge(exp_done, l * 4 * NS + 4 * s + 4)
                if STEPS[s][0] == "b":
                    dve.wait_ge(sink_exp_ready, l * 4 + (s - 2) + 1)
                    dve.tensor_tensor(row_sum[:, par, :], row_sum[:, par, :], sink_exp[:, par, :],
                                      ALU.add).then_inc(dve_step, own.one_more())
                    dve.wait_ge(dve_step, own.value(l))
                dve.reciprocal(row_inv[:, par, :], row_sum[:, par, :]).then_inc(dve_step, own.one_more())
                dve.wait_ge(dve_step, own.value(l))
                for n in range(4):
                    lo, w = (0, 256) if n < 2 else (256, 128)
                    cols = prob[:, par, 384 * (n % 2) + lo:384 * (n % 2) + lo + w]
                    ins = dve.tensor_scalar(cols, cols, row_inv[:, par, n:n + 1], None, ALU.mult)
                ins.then_inc(prob_ready, 1)

            def out_low(l, s):
                b, p = STEPS[s]
                kt = 4 * BRANCH_INDEX[b] + p
                dve.wait_ge(o_hi, l * NO + (s - 2) + 1)
                dve.tensor_tensor(br_lo[:, kt, :], bank[7][:, 0:SEQ], br_hi[:, kt, :].bitcast(F32),
                                  ALU.subtract).then_inc(o_lo, 1)

            def index_scores(l, own, s):
                dve.wait_ge(exp_done, l * 4 * NS + 4 * s + 4)
                for j in range(2):
                    h = 2 * s + j
                    for m, lo, w in ((1, 0, 256), (0, 256, 128)):
                        cols = score[:, lo:lo + w]
                        wt = proj[:, m, I_W + h:I_W + h + 1]
                        if h == 0:
                            dve.tensor_scalar(cols, relu_dots[:, h, lo:lo + w], wt, None,
                                              ALU.mult).then_inc(dve_step, own.one_more())
                        else:
                            dve.wait_ge(dve_step, own.value(l, own.n - 1))
                            dve.scalar_tensor_tensor(cols, relu_dots[:, h, lo:lo + w], wt, cols, ALU.mult,
                                                     ALU.add).then_inc(dve_step, own.one_more())

            def settled(l, own):
                dve.wait_ge(dve_step, own.value(l))
                dve.sem_inc(wait_passed, 1)

            def top_round(l, own):
                spans = ((0, 0, 256), (1, 256, 128))
                settled(l, own)
                for m, lo, w in spans:
                    dve.max(top8[:, m, :], picked[:, lo:lo + w]).then_inc(dve_step, own.one_more())
                settled(l, own)
                for m, lo, w in spans:
                    dve.match_replace(picked[:, lo:lo + w], top8[:, m, :], picked[:, lo:lo + w],
                                      TAKEN).then_inc(dve_step, own.one_more())

            with dve.Fori(0, LAYERS) as l:
                own = Count(DVE_PER_LAYER)
                low(l, 0)
                dve.wait_ge(small_in, l * 48 + 48)
                half_low(l, 0, 0, 0)
                low(l, 1)
                half_low(l, 0, 1, 0)
                low(l, 2)
                dve.tensor_scalar(sink_neg[:, :], sink_raw[:, :], -1.0, None,
                                  ALU.mult).then_inc(dve_step, own.one_more())
                low(l, 3)
                with dve.Fori(0, 2) as i:
                    for j in range(RING):
                        low(l, 4 + j, it=i)
                for u in range(K_OUT - K_STRAIGHT):
                    k = K_STRAIGHT + u
                    if 3 <= u <= NS:
                        maxima(l, own, u - 1)
                    low(l, k + 2)
                    if 1 <= u <= 2:
                        index_scores(l, own, u - 1)
                    if u == 2:
                        dve.wait_ge(mask_in, 16)
                        dve.wait_ge(dve_step, own.value(l))
                        dve.scalar_tensor_tensor(picked[:, :], mask_b[:, 0, :], MASKED, score[:, :],
                                                 ALU.mult, ALU.add).then_inc(dve_step, own.one_more())
                        dve.wait_ge(dve_step, own.value(l))
                        dve.sem_inc(chosen, 1)
                    if 4 <= u <= NS + 1:
                        take_probs(l, u - 2)
                    if 3 <= u < 3 + ROUNDS:
                        top_round(l, own)
                    if u == FIRST_A:
                        dve.wait_ge(dve_step, own.value(l))
                        dve.scalar_tensor_tensor(mask_b[:, 2, :], picked[:, :], TAKEN, mask_b[:, 0, :],
                                                 ALU.is_gt, ALU.add).then_inc(chosen, 1)
                    if 3 <= u <= NS:
                        normalise(l, own, u - 1)
                    if 4 <= u <= NS + 1:
                        out_low(l, u - 2)
                    if k >= K_BRANCH:
                        r = k - K_BRANCH
                        c, b = r // 3, BRANCH_INDEX[BRANCHES[r % 3]]
                        for m in range(MT):
                            dve.wait_ge(mm_done, half_no(l, k, m))
                            dve.wait_ge(proj_ready, proj_no(l, 2 * CHUNKS))
                            dst = merged[:, m, c * CW:(c + 1) * CW] if r % 3 == 0 else part[:, m, :]
                            if r % 3:
                                prior = 2 * (2 * c + r % 3 - 1) - 2 + m + 1
                                if prior > 0:
                                    dve.wait_ge(part_added, l * 8 + prior)
                            dve.scalar_tensor_tensor(dst, gate[:, m, b * D + c * CW:b * D + (c + 1) * CW], 1.0,
                                                     bank[2 * (r % 2) + m][:, :], ALU.add,
                                                     ALU.mult).then_inc(part_ready, 1)
                    if k == K_BRANCH + 4:
                        half_low(l, 1, 0, None)
                assert own.n == DVE_PER_LAYER, (own.n, DVE_PER_LAYER)
                low(l, K_OUT + 2)
                low(l, K_OUT + 3)
                half_low(l, 1, 1, None)
                low(l, K_OUT + 4)
                add_to_x(l, 0, K_OUT + 2, 0)
                low(l, K_OUT + 5)
                half_low(l, 2, 0, 1)
                add_to_x(l, 1, K_OUT + 3, 2)
                half_low(l, 2, 1, 1)

                def hidden_low(chunk, parity):
                    for b in range(2):
                        dve.wait_ge(act_t_hi, l * 2 * FFC + chunk * 2 + b + 1)
                        dve.tensor_tensor(act_lo[parity][:, 2 * b:2 * b + 2, :],
                                          bank[6 + b][:, :].rearrange("p (a n) -> p a n", a=2),
                                          act_hi[parity][:, 2 * b:2 * b + 2, :].bitcast(F32),
                                          ALU.subtract).then_inc(act_t_lo, 1)

                for j in range(3):
                    low(l, K_UP1 + j)
                hidden_low(0, 0)
                low(l, K_UP1 + 3)
                low(l, K_UP1 + 4)
                hidden_low(1, 1)
                low(l, K_UP1 + 5)
                with dve.Fori(0, MLP_ROUNDS) as i:
                    for a in range(2):
                        for j in range(3):
                            low(l, K_LOOP + RING * a + 2 + j, it=i * 2)
                        hidden_low(i * 2 + (2 + a), a)
                        low(l, K_LOOP + RING * a + 5, it=i * 2)
                add_to_x(l, 0, K_DOWN7, 4)
                add_to_x(l, 1, K_DOWN7 + 1, 2)
            dve.wait_ge(gf_in, 16)
            dve.wait_ge(x_ready, LAYERS * 8 + 4)
            dve.tensor_tensor(normed[:, 1, CW:D], xs[:, 1, CW:D], gain_f[:, CW:D], ALU.mult).then_inc(last_gained, 1)
            dve.wait_ge(gained, 3)
            dve.wait_ge(rstd_ready, 2 * LAYERS + 1)
            for c in range(2):
                cols = normed[:, 0, c * CW:(c + 1) * CW]
                dve.tensor_scalar(cols, cols, rstd[:, 0:1], None, ALU.mult).then_inc(y_ready, 1)
            dve.wait_ge(last_gained, 1)
            dve.wait_ge(rstd_ready, 2 * LAYERS + 2)
            cols = normed[:, 1, CW:D]
            dve.tensor_scalar(cols, cols, rstd[:, 1:2], None, ALU.mult).then_inc(y_ready, 1)

        @block.gpsimd
        def _(pool):
            for n, value in enumerate((-0.5, 0.5, EPS)):
                pool.memset(consts[:, n, :], value).then_inc(consts_set, 1)
            pool.wait_ge(consts_set, 3)
            pool.wait_ge(ident_in, 16)
            pool.tensor_scalar(ident_neg[:, :], ident[:, :], MASKED, None, ALU.mult).then_inc(const_ready, 1)
            pool.wait_ge(x_in[1], 16)
            pool.wait_ge(x_ready, 2)
            pool.sem_inc(x_ready, 2)
            pool.wait_ge(raw_in[0], 16)
            pool.dma_start(rope_sb[:, :, :, :], rope).then_inc(rope_in, 16)
            pool.dma_start(mask_b[:, 0:2, :], masks).then_inc(mask_in, 16)
            pool.wait_ge(rope_in, 16)

            def inverse_rms(count, done):
                pool.wait_ge(ssq_ready, count * 4)
                pool.tensor_tensor(var[:, 0, :], ssq[:, 0, :], ssq[:, 1, :], ALU.add).then_inc(pool_step, 1)
                pool.wait_ge(pool_step, done(1))
                pool.tensor_tensor(var[:, 1, :], var[:, 0, :], consts[:, 2, :], ALU.add).then_inc(pool_step, 1)
                pool.wait_ge(pool_step, done(2))
                pool.tensor_tensor(rstd[:, :], var[:, 1, :], consts[:, 0, :], ALU.pow).then_inc(pool_step, 1)
                pool.wait_ge(pool_step, done(3))
                pool.tensor_tensor(rstd_half[:, :], rstd[:, :], consts[:, 1, :], ALU.mult).then_inc(rstd_ready, 1)

            sections = ((A_Q, 9, ((8, 0),)), (I_Q, 5, ((4, 1),)), (B_Q, 10, ((8, 2), (9, 3))),
                        (C_Q, 8, ()), (C_K, 8, ()))
            with pool.Fori(0, LAYERS) as l:
                inverse_rms(l * 2 + 1, lambda n: l * POOL_PER_LAYER + n)
                for n, (col, heads, shared) in enumerate(sections):
                    chunks = 1 - (-(col + heads * HD - SHORT) // CW)
                    if n:
                        pool.wait_ge(rope_done, l * 5 + n)
                    pool.wait_ge(proj_ready, proj_no(l, 2 * chunks))
                    v = proj[:, :, col:col + heads * HD].rearrange("p m (h d) -> p m h d", d=HD)
                    t1 = rt1[:, 0:2 * heads * HD].rearrange("p (m h d) -> p m h d", m=MT, d=HD)
                    t2 = rt2[:, 0:2 * heads * HD].rearrange("p (m h d) -> p m h d", m=MT, d=HD)
                    cs = rope_sb[:, :, 0, :].unsqueeze(2).to_broadcast([P, MT, heads, HD])
                    sn = rope_sb[:, :, 1, :].unsqueeze(2)
                    half = HD // 2
                    pool.tensor_tensor(t1, v, cs, ALU.mult)
                    pool.tensor_tensor(t2[:, :, :, 0:half], v[:, :, :, half:HD],
                                       sn[:, :, :, 0:half].to_broadcast([P, MT, heads, half]), ALU.mult)
                    pool.tensor_tensor(t2[:, :, :, half:HD], v[:, :, :, 0:half],
                                       sn[:, :, :, half:HD].to_broadcast([P, MT, heads, half]),
                                       ALU.mult).then_inc(pool_step, 1)
                    pool.wait_ge(pool_step, l * POOL_PER_LAYER + (3 + n + 1))
                    for h, place in shared:
                        two = [P, MT, 2, HD]
                        pool.tensor_tensor(k_pair[:, place, :, :].rearrange("p m (t d) -> p m t d", t=2),
                                           t1[:, :, h, :].unsqueeze(2).to_broadcast(two),
                                           t2[:, :, h, :].unsqueeze(2).to_broadcast(two), ALU.add)
                    pool.tensor_tensor(v, t1, t2, ALU.add).then_inc(rope_done, 1)
                for r in range(6):
                    if r % 3 == 0:
                        continue
                    c = r // 3
                    for m in range(MT):
                        pool.wait_ge(part_ready, l * 12 + 2 * r + m + 1)
                        if r % 3 == 2:
                            pool.wait_ge(part_added, l * 8 + 4 * c + m + 1)
                        cols = merged[:, m, c * CW:(c + 1) * CW]
                        pool.tensor_tensor(cols, cols, part[:, m, :], ALU.add).then_inc(part_added, 1)
                inverse_rms(l * 2 + 2, lambda n: l * POOL_PER_LAYER + (8 + n))

                def square(chunk, first=False):
                    for m in range(MT):
                        pool.wait_ge(relu_ready, l * 2 * FFC + chunk * 2 + m + 1)
                        if not first:
                            pool.wait_ge(act_t, l * 2 * FFC + chunk * 2)
                        pool.tensor_tensor(up_sq[:, m, :], up_relu[:, m, :], up_relu[:, m, :],
                                           ALU.mult).then_inc(sq_ready, 1)

                square(0, first=True)
                square(1)
                with pool.Fori(0, MLP_ROUNDS) as i:
                    for a in range(2):
                        square(i * 2 + (2 + a))
            pool.wait_ge(gf_in, 16)
            for n, (c, m) in enumerate(((0, 0), (0, 1), (1, 0))):
                pool.wait_ge(x_ready, LAYERS * 8 + n + 1)
                cols = slice(c * CW, (c + 1) * CW)
                pool.tensor_tensor(normed[:, m, cols], xs[:, m, cols], gain_f[:, cols],
                                   ALU.mult).then_inc(gained, 1)
            for m in range(MT):
                steps = LAYERS * POOL_PER_LAYER + 2 * m
                tile = slice(m, m + 1)
                pool.wait_ge(ssq_ready, 8 * LAYERS + 3 + m)
                pool.tensor_tensor(var[:, 0, tile], ssq[:, 0, tile], ssq[:, 1, tile], ALU.add).then_inc(pool_step, 1)
                pool.wait_ge(pool_step, steps + 1)
                pool.tensor_tensor(var[:, 1, tile], var[:, 0, tile], consts[:, 2, tile],
                                   ALU.add).then_inc(pool_step, 1)
                pool.wait_ge(pool_step, steps + 2)
                pool.tensor_tensor(rstd[:, tile], var[:, 1, tile], consts[:, 0, tile],
                                   ALU.pow).then_inc(rstd_ready, 1)

        @block.tensor
        def _(pe):
            pe.wait_ge(zero_ready, 1)
            for n in range(WARM_UP):
                pe.matmul(bank[2][:, :], zeros[:, 0:P], zeros[:, :], start=True, stop=True)
            pe.wait_ge(ident_in, 16)
            pe.sem_inc(mm_done, 2 * RING)

            def unit(l, k, left_hi, left_lo, banks, first, last, it=None, free=None, pauses=None, left=None):
                slot, n, width = k % RING, 0, width_of(k, it)
                pe.wait_ge(lo_ready, unit_no(l, k, it) + 1 + RAW)
                for m in range(MT):
                    if free:
                        free(m)
                    for kt in range(KU):
                        if left and m == 0 and kt % 2 == 0:
                            left(kt // 2)
                        rows = slice(m * P, (m + 1) * P)
                        for p, (a, w) in enumerate(((left_hi, w_hi), (left_hi, w_lo), (left_lo, w_hi))):
                            if pauses and n % 4 == 0 and n // 4 in pauses:
                                pauses[n // 4]()
                            n += 1
                            ins = pe.matmul(bank[banks + m][:, 0:width], a[:, kt, rows],
                                            w[:, slot, kt, 0:width],
                                            start=first and kt == 0 and p == 0,
                                            stop=last and kt == KU - 1 and p == 2)
                    ins.then_inc(mm_done, 1)

            def rows_of(t, n):
                return t[:, KU * n:KU * (n + 1), :]

            def transpose_half(l, group, c, src):
                for b in range(2):
                    for a in range(2):
                        for m in range(MT):
                            kt = 4 * c + 2 * b + a
                            ins = pe.transpose(bank[(6, 4)[c] + b][:, a * SEQ + m * P:a * SEQ + (m + 1) * P],
                                               src[:, m, kt * P:(kt + 1) * P], ident[:, :])
                    ins.then_inc(half_t, 1)

            def t_job(l, kind, step):
                j = T_JOBS.index((kind, step))
                b, p = STEPS[step]
                if j:
                    pe.wait_ge(t_taken, l * NT + j)
                pe.wait_ge(rope_done, l * 5 + {"i": 2, "b": 3, "c": 5, "a": 5}[b])
                for m in range(MT):
                    if kind == "q":
                        src = proj[:, m, Q_COL[b] + P * p:Q_COL[b] + P * (p + 1)]
                    else:
                        col, heads = key_of(step)
                        if heads == 2:
                            src = proj[:, m, col:col + P]
                        else:
                            src = k_pair[:, {A_K: 0, I_K: 1, B_K: 2, B_K + HD: 3}[col], m, :]
                    ins = pe.transpose(bank[6][:, m * P:(m + 1) * P], src, ident[:, :])
                ins.then_inc(t_done, 1)

            def scores(l, s):
                b, p = STEPS[s]
                q_job = T_JOBS.index(("q", s))
                jobs = [q_job] + [T_JOBS.index(("k", x)) for x in range(s + 1) if key_of(x)][-1:]
                pe.wait_ge(t_taken, l * NT + max(jobs) + 1)
                if s:
                    pe.wait_ge(exp_done, l * 4 * NS + 4 * s)
                if s == FIRST_A:
                    pe.wait_ge(chosen, l * 2 + 2)
                kb = k_t[:, KEY_JOB[s] % 2, :]
                if b != "i":
                    if s == 2:
                        pe.wait_ge(const_ready, 1)
                        pe.wait_ge(mask_in, 16)
                    for j in range(2):
                        pe.matmul(bank[2 + j][:, 0:384], ident_neg[:, :],
                                  mask_b[:, {"c": 0, "b": 1, "a": 2}[b], :], start=True, stop=False)
                for m, keys, lo in ((1, 256, 0), (0, 128, 256)):
                    for j in range(2):
                        rows = slice(HD * j, HD * j + HD)
                        ins = pe.matmul(bank[2 + j][:, lo:lo + keys],
                                        q_t[rows, s % 2, m * P:(m + 1) * P], kb[rows, 0:keys],
                                        start=b == "i", stop=b == "i" or m == 0)
                        if m == 0:
                            ins.then_inc(s_done, 1)

            def transpose_probs(l, s):
                par = s % 2
                pe.wait_ge(prob_ready, l * NO + (s - 2) + 1)
                if s > 2:
                    pe.wait_ge(pt1_taken, l * NO + s - 2)
                    pe.wait_ge(pt0_taken, l * NO + s - 2)
                for n in range(6):
                    dst = bank[4][:, n * P:(n + 1) * P] if n < 4 else bank[5][:, (n - 4) * P:(n - 3) * P]
                    at = 3 * (n // 3) + (2, 0, 1)[n % 3]
                    ins = pe.transpose(dst, prob[:, par, at * P:(at + 1) * P], ident[:, :])
                    if n in (3, 5):
                        ins.then_inc(pt_done, 1)

            def values(l, s):
                b, p = STEPS[s]
                pe.wait_ge(pt1_taken, l * NO + s - 1)
                pe.wait_ge(pt0_taken, l * NO + s - 1)
                if b == "c":
                    pe.wait_ge(proj_ready, proj_no(l, 2 * QKV_CHUNKS))
                if s > 2:
                    pe.wait_ge(o_lo, l * NO + s - 2)
                for kb in range(2):
                    for j in range(2):
                        col = value_col(b, 2 * p + j)
                        lo, w = ((0, SEQ), (P, P))[kb]
                        ins = pe.matmul(bank[7][HD * j:HD * (j + 1), lo:lo + w], proj[:, kb, col:col + HD],
                                        prob_t[:, 384 * j + 2 * P * kb:384 * j + 2 * P * kb + w],
                                        start=kb == 0, stop=kb == 1)
                ins.then_inc(pv_done, 1)

            with pe.Fori(0, LAYERS) as l:
                pe.wait_ge(x_ready, l * 8 + 2)
                transpose_half(l, 0, 0, xs)
                for r in range(2):
                    pauses = {}
                    if r == 0:
                        def x_half():
                            pe.wait_ge(x_ready, l * 8 + 4)
                            transpose_half(l, 0, 1, xs)
                        pauses[1] = x_half

                    def left(b):
                        pe.wait_ge(half_lo, l * 12 + 2 * r + b + 1)
                    unit(l, r, rows_of(h_hi, r), rows_of(h_lo, r), 0, r == 0, r == 1,
                         pauses=pauses, left=left)
                with pe.Fori(0, 2) as i:
                    for j in range(RING):
                        banks = 2 - 2 * (j // 2)

                        def free(m, j=j):
                            if j == 0:
                                pe.wait_ge(proj_ready, proj_no(l, 0) + i * 4)
                            if j == 2:
                                pe.wait_ge(proj_ready, proj_no(l, m + 1) + i * 4)
                        unit(l, 2 + j, rows_of(h_hi, j % 2), rows_of(h_lo, j % 2), banks, j % 2 == 0, j % 2 == 1,
                             it=i, free=free)
                for u in range(K_OUT - K_STRAIGHT):
                    k = K_STRAIGHT + u
                    pauses = {}
                    if 1 <= u <= NS:
                        pauses[0] = lambda: scores(l, u - 1)
                    if u < NS:
                        pauses[1] = lambda: t_job(l, "q", u)
                        if key_of(u):
                            pauses[3] = lambda: t_job(l, "k", u)
                    if 4 <= u <= NS + 1:
                        pauses[2] = lambda: transpose_probs(l, u - 2)
                        pauses[4] = lambda: values(l, u - 2)
                    if k < K_BRANCH:
                        e, r = k // 2, k % 2

                        def free(m):
                            if r == 0:
                                pe.wait_ge(proj_ready, proj_no(l, 2 * (e - 1) + m + 1))
                        unit(l, k, rows_of(h_hi, r), rows_of(h_lo, r), 0, r == 0, r == 1, free=free, pauses=pauses)
                        continue
                    r = k - K_BRANCH
                    b = BRANCH_INDEX[BRANCHES[r % 3]]
                    if r == 1:
                        pe.wait_ge(exp_done, (l + 1) * (4 * NS))
                    if r < 3:
                        pe.wait_ge(o_lo, l * NO + 4 * (r + 1))

                    def free(m):
                        if r == 0:
                            pe.wait_ge(proj_ready, proj_no(l, 2 * CHUNKS - 1 + m))
                        if r >= 2:
                            pe.wait_ge(part_ready, l * 12 + 2 * (r - 2) + m + 1)
                    if r == 4:
                        def merged_half():
                            pe.wait_ge(part_added, l * 8 + 4)
                            transpose_half(l, 1, 0, merged)
                        pauses[3] = merged_half
                    unit(l, k, rows_of(br_hi, b), rows_of(br_lo, b), 2 * (r % 2), True, True, free=free,
                         pauses=pauses)
                for r in range(4):
                    pauses = {}
                    if r == 1:
                        def merged_half():
                            pe.wait_ge(part_added, l * 8 + 8)
                            transpose_half(l, 1, 1, merged)
                        pauses[2] = merged_half
                    if r == 3:
                        def x_half():
                            pe.wait_ge(x_ready, l * 8 + 6)
                            transpose_half(l, 2, 0, xs)
                        pauses[2] = x_half

                    def free(m):
                        if r < 2:
                            pe.wait_ge(part_ready, l * 12 + 8 + 2 * r + m + 1)

                    def left(b):
                        if r % 2 == 0:
                            pe.wait_ge(half_lo, l * 12 + 4 + r + b + 1)
                    unit(l, K_OUT + r, rows_of(h_hi, r // 2), rows_of(h_lo, r // 2), 2 * (r % 2), r < 2, r >= 2,
                         free=free, pauses=pauses, left=left)
                def up(k, chunk, it=None, pause=None, first_chunk=False, banks=0):
                    for r in range(2):
                        pauses = {}
                        if first_chunk and r == 0:
                            def x_half():
                                pe.wait_ge(x_ready, l * 8 + 8)
                                transpose_half(l, 2, 1, xs)
                            pauses[3] = x_half
                        if r == 1 and pause:
                            pauses[0] = pause

                        def free(m):
                            if r == 0 and not first_chunk and banks == 0:
                                pe.wait_ge(relu_ready, l * 2 * FFC + chunk * 2)

                        def left(b):
                            if first_chunk:
                                pe.wait_ge(half_lo, l * 12 + 8 + 2 * r + b + 1)
                        unit(l, k + r, rows_of(h_hi, r), rows_of(h_lo, r), banks, r == 0, r == 1, it=it, free=free,
                             pauses=pauses, left=left)

                def transpose_hidden(chunk):
                    pe.wait_ge(sq_ready, l * 2 * FFC + chunk * 2 + 2)
                    for b in range(2):
                        for a in range(2):
                            for m in range(MT):
                                kt = 2 * b + a
                                ins = pe.transpose(bank[6 + b][:, a * SEQ + m * P:a * SEQ + (m + 1) * P],
                                                   up_sq[:, m, kt * P:(kt + 1) * P], ident[:, :])
                        ins.then_inc(act_t, 1)

                def down(k, chunk, parity, it=None, first=False, last=False):
                    for r in range(2):
                        def left(b):
                            if r == 0:
                                pe.wait_ge(act_t_lo, l * 2 * FFC + chunk * 2 + b + 1)

                        def free(m):
                            if r == 1 and first:
                                pe.wait_ge(relu_ready, l * 2 * FFC + 4)
                        pauses = {}
                        if r == 1 and not last:
                            pauses[0] = lambda: transpose_hidden(chunk + 1)
                        unit(l, k + r, act_hi[parity], act_lo[parity], 4 - 2 * r, first, last, it=it,
                             free=free, pauses=pauses, left=left)

                up(K_UP0, 0, first_chunk=True)
                up(K_UP1, 1, banks=2, pause=lambda: transpose_hidden(0))
                down(K_UP1 + 2, 0, 0, first=True)
                with pe.Fori(0, MLP_ROUNDS) as i:
                    for a in range(2):
                        up(K_LOOP + RING * a, i * 2 + (2 + a), it=i * 2)
                        down(K_LOOP + RING * a + 2, i * 2 + (1 + a), 1 - a, it=i * 2)
                down(K_DOWN7, FFC - 1, (FFC - 1) % 2, last=True)


def rotation_table():
    import numpy as np
    inv = 1.0 / (np.float32(10000.0) ** (np.arange(0, HD, 2, dtype=np.float32) / np.float32(HD)))
    angle = np.arange(SEQ, dtype=np.float32)[:, None] * inv.astype(np.float32)[None, :]
    c, s = np.cos(angle), np.sin(angle)
    table = np.stack([np.concatenate([c, c], 1), np.concatenate([-s, s], 1)], 1)
    return np.ascontiguousarray(table.reshape(MT, P, 2, HD).transpose(1, 0, 2, 3).astype(np.float32))


def mask_table():
    import numpy as np
    row, key = np.arange(P)[:, None], np.arange(SEQ)[None, :]
    table = np.zeros((P, 2, 384), np.float32)
    for at, m, keys in ((0, 1, 256), (256, 0, 128)):
        diff = (row + m * P) - key[:, :keys]
        table[:, 0, at:at + keys] = diff < 0
        table[:, 1, at:at + keys] = (diff < 0) | (diff >= 128)
    return table


def kernel(x, norm1, w_in, sinks, w_branch, w_out, norm2, w_ff1, w_ff2, norm_f):
    import numpy as np
    import concourse.bacc as bacc
    from concourse.bass_utils import run_bass_kernel_spmd

    def features_on_rows(a):
        return a.reshape(LAYERS, KT, P).transpose(2, 0, 1).reshape(P, LAYERS * KT)

    nc = bacc.Bacc("TRN2", target_bir_lowering=False, num_devices=1)
    given = {"x": x, "norm1": features_on_rows(np.asarray(norm1)), "w_in": w_in,
             "sinks": sinks, "w_branch": w_branch, "w_out": w_out,
             "norm2": features_on_rows(np.asarray(norm2)), "w_ff1": w_ff1, "w_ff2": w_ff2, "norm_f": norm_f,
             "rope": rotation_table(), "masks": mask_table(), "identity": np.eye(P, dtype=np.float32)}
    arrays = {f"in_{n}": np.ascontiguousarray(a) for n, a in given.items()}
    aps = [nc.dram_tensor(n, a.shape, mybir.dt.from_np(a.dtype), kind="ExternalInput").ap()
           for n, a in arrays.items()]
    out = nc.dram_tensor("out_0", (1, SEQ, D), F32, kind="ExternalOutput").ap()
    program(nc, *aps, out)
    result = run_bass_kernel_spmd(nc, [arrays], core_ids=[0])
    return result.results[0]["out_0"]
```
